# Optimizing a Trainium2 kernel written in Bass

```python
import jax, jax.numpy as jnp
from jax import lax
import numpy as np

D_MODEL = 1024
BATCH = 1
SEQ = 512
DEPTH = 2

EPS = 1e-6
MLSTM_HEADS = 4
MLSTM_HEAD_DIM = 128
MLSTM_WIDTH = MLSTM_HEADS * MLSTM_HEAD_DIM
MLSTM_CHUNK = 128
CONV_GROUPS = 4
CONV_CH = D_MODEL // 2
CONV_K = 3
IN0_WIDTH = 4 * MLSTM_WIDTH + 2 * MLSTM_HEADS + 3 * CONV_CH
MIX0_WIDTH = MLSTM_WIDTH + CONV_CH
SB_HEADS = 16
SB_HEAD_DIM = D_MODEL // SB_HEADS
SB_BLOCK = 128
PEER_HEADS = 8
PEER_NKEYS = 128
PEER_EXPERTS = PEER_NKEYS * PEER_NKEYS
PEER_QDIM = 256
PEER_HALF = PEER_QDIM // 2
PEER_TOPK = 16
PEER_TOKEN_BLOCK = 128

kernel_name = "hybrid_mlstm_conv_stickbreak_peer"

def rmsnorm(x, g):
    xf = x.astype(jnp.float32)
    y = xf * lax.rsqrt(jnp.mean(xf * xf, axis=-1, keepdims=True) + EPS)
    return (y * g.astype(jnp.float32)).astype(x.dtype)

def ada_params(c, w, b):
    mod = jnp.einsum("bd,de->be", jax.nn.silu(c), w) + b
    return jnp.split(mod, 6, axis=-1)

def modulate(x, g, shift, scale):
    return rmsnorm(x, g) * (1 + scale[:, None, :]) + shift[:, None, :]

def mlstm_chunkwise(q, k, v, i_pre, f_pre):
    B, H, S, dh = q.shape
    L = MLSTM_CHUNK
    NC = S // L
    f32 = jnp.float32
    qc = (q.astype(f32) * dh ** -0.5).reshape(B, H, NC, L, dh)
    kc = k.astype(f32).reshape(B, H, NC, L, dh)
    vc = v.astype(f32).reshape(B, H, NC, L, dh)
    log_f = jax.nn.log_sigmoid(f_pre.astype(f32)).reshape(B, H, NC, L)
    log_i = i_pre.astype(f32).reshape(B, H, NC, L)
    b = jnp.cumsum(log_f, axis=-1)
    g_chunk = b[..., -1]
    a = g_chunk[..., None] - b + log_i

    def step(carry, inp):
        s_, n_, m_ = carry
        k_, v_, a_, g_ = inp
        m_new = jnp.maximum(g_ + m_, jnp.max(a_, axis=-1))
        decay = jnp.exp(g_ + m_ - m_new)
        w = jnp.exp(a_ - m_new[..., None])
        s_new = decay[..., None, None] * s_ + jnp.einsum("bhl,bhld,bhle->bhde", w, k_, v_)
        n_new = decay[..., None] * n_ + jnp.einsum("bhl,bhld->bhd", w, k_)
        return (s_new, n_new, m_new), (s_, n_, m_)

    init = (jnp.zeros((B, H, dh, dh), f32), jnp.zeros((B, H, dh), f32), jnp.zeros((B, H), f32))
    xs = (jnp.moveaxis(kc, 2, 0), jnp.moveaxis(vc, 2, 0), jnp.moveaxis(a, 2, 0), jnp.moveaxis(g_chunk, 2, 0))
    _, (s_prev, n_prev, m_prev) = lax.scan(step, init, xs)
    s_prev = jnp.moveaxis(s_prev, 0, 2)
    n_prev = jnp.moveaxis(n_prev, 0, 2)
    m_prev = jnp.moveaxis(m_prev, 0, 2)

    causal = jnp.tril(jnp.ones((L, L), dtype=bool))
    log_d = jnp.where(causal, b[..., :, None] - b[..., None, :] + log_i[..., None, :], -jnp.inf)
    inter_log = b + m_prev[..., None]
    m_t = jnp.maximum(inter_log, jnp.max(log_d, axis=-1))
    qk = jnp.einsum("bhcld,bhcsd->bhcls", qc, kc) * jnp.exp(log_d - m_t[..., None])
    inter_w = jnp.exp(inter_log - m_t)
    num = jnp.einsum("bhcls,bhcsd->bhcld", qk, vc) + inter_w[..., None] * jnp.einsum("bhcld,bhcde->bhcle", qc, s_prev)
    den = jnp.sum(qk, axis=-1) + inter_w * jnp.einsum("bhcld,bhcd->bhcl", qc, n_prev)
    h = num / jnp.maximum(jnp.abs(den), jnp.exp(-m_t))[..., None]
    return h.reshape(B, H, S, dh).astype(q.dtype)

def mlstm_conv_mixer(h, w_in, b_igate, b_fgate, conv_w, mlstm_norm, w_out):
    B, S, _ = h.shape
    W, Hn, dh = MLSTM_WIDTH, MLSTM_HEADS, MLSTM_HEAD_DIM
    proj = jnp.einsum("bsd,de->bse", h, w_in)
    cuts = [W, 2 * W, 3 * W, 4 * W, 4 * W + Hn, 4 * W + 2 * Hn,
            4 * W + 2 * Hn + CONV_CH, 4 * W + 2 * Hn + 2 * CONV_CH]
    q, k, v, o, gi, gf, cb, cc, ch = jnp.split(proj, cuts, axis=-1)

    def heads(t):
        return t.reshape(B, S, Hn, dh).transpose(0, 2, 1, 3)

    hm = mlstm_chunkwise(heads(q), heads(k), heads(v),
                         (gi + b_igate).transpose(0, 2, 1), (gf + b_fgate).transpose(0, 2, 1))
    hm = rmsnorm(hm.transpose(0, 2, 1, 3), mlstm_norm.reshape(Hn, dh))
    hm = hm.reshape(B, S, W) * jax.nn.sigmoid(o)
    u = cc * ch
    conv = lax.conv_general_dilated(u, conv_w[:, None, :], window_strides=(1,),
                                    padding=[(CONV_K - 1, 0)],
                                    dimension_numbers=("NWC", "WIO", "NWC"),
                                    feature_group_count=CONV_CH)
    hc = cb * conv
    return jnp.einsum("bse,ed->bsd", jnp.concatenate([hm, hc], axis=-1), w_out)

def stick_breaking_mixer(h, w_qkv, q_norm, k_norm, w_out):
    B, S, _ = h.shape
    f32 = jnp.float32
    qkv = jnp.einsum("bsd,de->bse", h, w_qkv).reshape(B, S, 3, SB_HEADS, SB_HEAD_DIM)
    q = rmsnorm(qkv[:, :, 0], q_norm).astype(f32).transpose(0, 2, 1, 3)
    k = rmsnorm(qkv[:, :, 1], k_norm).astype(f32).transpose(0, 2, 1, 3)
    v = qkv[:, :, 2].astype(f32).transpose(0, 2, 1, 3)
    scale = SB_HEAD_DIM ** -0.5
    outs = []
    for blk in range(S // SB_BLOCK):
        q0 = blk * SB_BLOCK
        kend = q0 + SB_BLOCK
        z = jnp.einsum("bhtd,bhsd->bhts", q[:, :, q0:kend], k[:, :, :kend]) * scale
        strict = jnp.arange(kend)[None, :] < (q0 + jnp.arange(SB_BLOCK))[:, None]
        log_1mb = jnp.where(strict, jax.nn.log_sigmoid(-z), 0.0)
        between = lax.cumsum(log_1mb, axis=3, reverse=True) - log_1mb
        att = jnp.where(strict, jnp.exp(jax.nn.log_sigmoid(z) + between), 0.0)
        outs.append(jnp.einsum("bhts,bhsd->bhtd", att, v[:, :, :kend]))
    o = jnp.concatenate(outs, axis=2).transpose(0, 2, 1, 3).reshape(B, S, D_MODEL).astype(h.dtype)
    return jnp.einsum("bse,ed->bsd", o, w_out)

def peer_ffn(h, w_query, sub_keys1, sub_keys2, expert_u, expert_v):
    B, S, D = h.shape
    K = PEER_TOPK
    q = jnp.einsum("bsd,de->bse", h, w_query).reshape(B, S, PEER_HEADS, 2, PEER_HALF)
    s1 = jnp.einsum("bshd,nd->bshn", q[..., 0, :], sub_keys1)
    s2 = jnp.einsum("bshd,nd->bshn", q[..., 1, :], sub_keys2)
    v1, i1 = lax.top_k(s1, K)
    v2, i2 = lax.top_k(s2, K)
    cand = (v1[..., :, None] + v2[..., None, :]).reshape(B, S, PEER_HEADS, K * K)
    top_v, top_i = lax.top_k(cand, K)
    e1 = jnp.take_along_axis(i1, top_i // K, axis=-1)
    e2 = jnp.take_along_axis(i2, top_i % K, axis=-1)
    expert = e1 * PEER_NKEYS + e2
    gate = jax.nn.softmax(top_v.astype(jnp.float32), axis=-1).astype(h.dtype)
    nb = (B * S) // PEER_TOKEN_BLOCK
    xb = h.reshape(nb, PEER_TOKEN_BLOCK, D)
    eb = expert.reshape(nb, PEER_TOKEN_BLOCK, PEER_HEADS, K)
    gb = gate.reshape(nb, PEER_TOKEN_BLOCK, PEER_HEADS, K)

    def block(args):
        xt, et, gt = args
        act = jax.nn.gelu(jnp.einsum("td,thkd->thk", xt, expert_u[et]), approximate=False) * gt
        return jnp.einsum("thk,thkd->td", act, expert_v[et])

    return lax.map(block, (xb, eb, gb)).reshape(B, S, D)

def setup_inputs(seed: int = 0) -> dict:
    key = jax.random.key(seed)
    ks = iter(jax.random.split(key, 40))
    nrm = lambda shape, s: jax.random.normal(next(ks), shape, jnp.float32) * s
    gain = lambda n: 1.0 + 0.02 * jax.random.normal(next(ks), (n,), jnp.float32)
    D = D_MODEL
    inp = {}
    inp["x"] = nrm((BATCH, SEQ, D), 1.0)
    inp["c"] = nrm((BATCH, D), 1.0)
    inp["l0_ada_w"] = nrm((D, 6 * D), 0.2 * D ** -0.5)
    inp["l0_ada_b"] = nrm((6 * D,), 0.01)
    inp["l0_norm_mix"] = gain(D)
    inp["l0_w_in"] = nrm((D, IN0_WIDTH), D ** -0.5)
    inp["l0_b_igate"] = nrm((MLSTM_HEADS,), 0.5)
    inp["l0_b_fgate"] = jnp.linspace(3.0, 6.0, MLSTM_HEADS, dtype=jnp.float32) + nrm((MLSTM_HEADS,), 0.1)
    inp["l0_conv_w"] = nrm((CONV_K, CONV_CH), CONV_K ** -0.5)
    inp["l0_mlstm_norm"] = gain(MLSTM_WIDTH)
    inp["l0_w_out"] = nrm((MIX0_WIDTH, D), MIX0_WIDTH ** -0.5)
    inp["l0_norm_ffn"] = gain(D)
    inp["l0_peer_wq"] = nrm((D, PEER_HEADS * PEER_QDIM), D ** -0.5)
    inp["l0_peer_k1"] = nrm((PEER_NKEYS, PEER_HALF), PEER_HALF ** -0.5)
    inp["l0_peer_k2"] = nrm((PEER_NKEYS, PEER_HALF), PEER_HALF ** -0.5)
    inp["l0_peer_u"] = nrm((PEER_EXPERTS, D), D ** -0.5)
    inp["l0_peer_v"] = nrm((PEER_EXPERTS, D), PEER_HEADS ** -0.5)
    inp["l1_ada_w"] = nrm((D, 6 * D), 0.2 * D ** -0.5)
    inp["l1_ada_b"] = nrm((6 * D,), 0.01)
    inp["l1_norm_mix"] = gain(D)
    inp["l1_w_qkv"] = nrm((D, 3 * D), D ** -0.5)
    inp["l1_q_norm"] = gain(SB_HEAD_DIM)
    inp["l1_k_norm"] = gain(SB_HEAD_DIM)
    inp["l1_w_out"] = nrm((D, D), D ** -0.5)
    inp["l1_norm_ffn"] = gain(D)
    inp["l1_peer_wq"] = nrm((D, PEER_HEADS * PEER_QDIM), D ** -0.5)
    inp["l1_peer_k1"] = nrm((PEER_NKEYS, PEER_HALF), PEER_HALF ** -0.5)
    inp["l1_peer_k2"] = nrm((PEER_NKEYS, PEER_HALF), PEER_HALF ** -0.5)
    inp["l1_peer_u"] = nrm((PEER_EXPERTS, D), D ** -0.5)
    inp["l1_peer_v"] = nrm((PEER_EXPERTS, D), PEER_HEADS ** -0.5)
    return inp

def reference(x, c,
              l0_ada_w, l0_ada_b, l0_norm_mix, l0_w_in, l0_b_igate, l0_b_fgate, l0_conv_w,
              l0_mlstm_norm, l0_w_out, l0_norm_ffn, l0_peer_wq, l0_peer_k1, l0_peer_k2,
              l0_peer_u, l0_peer_v,
              l1_ada_w, l1_ada_b, l1_norm_mix, l1_w_qkv, l1_q_norm, l1_k_norm, l1_w_out,
              l1_norm_ffn, l1_peer_wq, l1_peer_k1, l1_peer_k2, l1_peer_u, l1_peer_v):
    layers = [
        dict(ada_w=l0_ada_w, ada_b=l0_ada_b, norm_mix=l0_norm_mix, norm_ffn=l0_norm_ffn,
             peer=(l0_peer_wq, l0_peer_k1, l0_peer_k2, l0_peer_u, l0_peer_v),
             mix=(l0_w_in, l0_b_igate, l0_b_fgate, l0_conv_w, l0_mlstm_norm, l0_w_out)),
        dict(ada_w=l1_ada_w, ada_b=l1_ada_b, norm_mix=l1_norm_mix, norm_ffn=l1_norm_ffn,
             peer=(l1_peer_wq, l1_peer_k1, l1_peer_k2, l1_peer_u, l1_peer_v),
             mix=(l1_w_qkv, l1_q_norm, l1_k_norm, l1_w_out)),
    ]
    for layer in range(DEPTH):
        p = layers[layer]
        sh1, sc1, g1, sh2, sc2, g2 = ada_params(c, p["ada_w"], p["ada_b"])
        h = modulate(x, p["norm_mix"], sh1, sc1)
        if layer % 2 == 0:
            y = mlstm_conv_mixer(h, *p["mix"])
        else:
            y = stick_breaking_mixer(h, *p["mix"])
        x = x + (1 + g1)[:, None, :] * y
        h = modulate(x, p["norm_ffn"], sh2, sc2)
        x = x + (1 + g2)[:, None, :] * peer_ffn(h, *p["peer"])
    return x


_drawn_inputs = setup_inputs


def setup_inputs(seed=0):
    import zlib

    import numpy as np

    out = dict(_drawn_inputs(seed))
    spreads = {}
    factors = {'l0_b_igate': 43.312,
     'l0_mlstm_norm': 2.868,
     'l1_ada_b': 2.75,
     'l1_norm_mix': 3.281,
     'l1_q_norm': 6.577,
     'l1_k_norm': 6.454,
     'l1_norm_ffn': 10.156}
    for name, (base, spread) in spreads.items():
        noise = np.random.default_rng([zlib.crc32(name.encode()), seed]).standard_normal(out[name].shape)
        drawn = base * np.exp(spread * noise) if base else spread * noise
        out[name] = __import__('jax').numpy.asarray(drawn.astype(out[name].dtype))
    for name, factor in factors.items():
        out[name] = (out[name] * factor).astype(out[name].dtype)
    return out
```

```python
from contextlib import ExitStack

import concourse.bass as bass
from concourse import mybir

F32 = mybir.dt.float32
F32R = mybir.dt.float32r
BF16 = mybir.dt.bfloat16
U32 = mybir.dt.uint32
ALU = mybir.AluOpType
ACT = mybir.ActivationFunctionType
AX_X = mybir.AxisListType.X
ds = bass.ds

P = 128
SEQ = 512
D = 1024
DC = D // P
EPS = 1e-6
CH = SEQ // P
HEADS = 4
SB_HEADS = 16
HD = D // SB_HEADS
PH = 8
TOPK = 16
NKEYS = 128
GROUP = 8
NGROUP = NKEYS // GROUP
UNIT = 4
BATCH = 64
NBATCH = SEQ // BATCH
LOWEST = -3.0e38
MASKED = -1.0e30
NO_SIGN = 0x7FFFFFFF

N_IN = 29
N_OUT = DC
N_WQ = 2 * PH
N_DENSE = 2 * NKEYS
N_QKV = 3 * DC
IN0 = 0
OUT0 = IN0 + N_IN
WQ0 = OUT0 + N_OUT
DENSE0 = WQ0 + N_WQ
QKV1 = DENSE0 + N_DENSE
OUT1 = QKV1 + N_QKV
WQ1 = OUT1 + N_OUT
DENSE1 = WQ1 + N_WQ
N_TILES = DENSE1 + N_DENSE
WQ = (WQ0, WQ1)
DENSE = (DENSE0, DENSE1)
OUTP = (OUT0, OUT1)
RING = 4
LEAD = 3
ADA = 6 * DC


def evacuators():
    dense = "a" * GROUP + ("a" * GROUP + "d" * GROUP) * (NGROUP - 1) + "d" * GROUP
    layer = "d" * N_OUT + "a" * N_WQ + dense
    return "a" * N_IN + layer + "a" * N_QKV + layer


EVAC = evacuators()
assert len(EVAC) == N_TILES


def emptied(kind, t):
    return EVAC[:t + 1].count(kind)


def build(nc, stream, x_t, c, ada, ada_b, gains, gate_b, conv_w, mnorm, keys, qk_norm, out_t):
    ctx = ExitStack()
    base = -(-nc.sbuf_base // 64) * 64
    limit = nc.sbuf_usable_end
    place = [base]

    def sb(name, shape, dt=F32):
        size = mybir.dt.size(dt)
        for n in shape[1:]:
            size *= n
        t = nc.alloc_sbuf_tensor_at(name, shape, dt, offset=place[0])
        place[0] += -(-size // 64) * 64
        assert place[0] <= limit, (name, place[0], limit)
        return t

    ident = sb("ident", [P, P])
    identb = sb("identb", [P, P], BF16)
    ones = sb("ones", [P, P])
    halfones = sb("halfones", [P, P])
    negtri = sb("negtri", [P, P])
    negones = sb("negones", [P, P])
    masked = sb("masked", [P, P], BF16)
    causal = sb("causal", [P, P])
    rowsel = sb("rowsel", [HEADS, HEADS, P])
    iota = sb("iota", [P, P])
    mod = sb("mod", [P, 2, ADA])
    adab = sb("adab", [P, 2, ADA])
    gain = sb("gain", [P, 4, DC])
    scol = sb("scol", [P, 4, DC])
    g1p = sb("g1p", [P, 4, DC])
    gateb = sb("gateb", [HEADS, 2])
    convw = sb("convw", [P, HEADS, 3])
    mnormc = sb("mnormc", [P, HEADS])
    qkn = sb("qkn", [P, 2])
    keysT = sb("keysT", [P, 2, 2, NKEYS])
    cvec = sb("cvec", [P, D])
    adacol = sb("adacol", [P, 2])
    grant = sb("grant", [P, 1])
    ada_w = sb("ada_w", [P, 2, D])
    raw = sb("raw", [P, RING, D])
    w_hi = sb("w_hi", [P, RING, D], F32R)
    w_lo = sb("w_lo", [P, RING, D], F32R)
    xT = sb("xT", [P, DC, SEQ])
    h_hi = sb("h_hi", [P, DC, SEQ], F32R)
    h_lo = sb("h_lo", [P, DC, SEQ], F32R)
    arena = place[0]

    KB = 1024
    ada_first = sb("ada_first", [P, 2 * DC, D])

    place[0] = arena + 64 * KB
    sq = sb("sq", [P, 2, SEQ])
    acc = sb("acc", [P, SEQ])
    rstd = sb("rstd", [P, SEQ])
    hw = sb("hw", [P, 2, SEQ])

    place[0] = arena
    qT = sb("qT", [P, HEADS, SEQ])
    kT = sb("kT", [P, HEADS, SEQ])
    vT = sb("vT", [P, HEADS, SEQ])
    oT = sb("oT", [P, HEADS, SEQ])
    rows_at = place[0]
    cbT = sb("cbT", [P, HEADS, SEQ])
    ccT = sb("ccT", [P, HEADS, SEQ])
    chT = sb("chT", [P, HEADS, SEQ])
    li = sb("li", [HEADS, CH, P])
    lf = sb("lf", [HEADS, CH, P])
    v_nat = sb("v_nat", [P, CH, 2 * P])
    k_nat = sb("k_nat", [P, CH - 1, P])
    state = sb("state", [P, CH - 1, 2 * P])
    gcols = sb("gcols", [P, 2, CH, HEADS])
    decay_b = sb("decay_b", [P, HEADS, CH])
    small = sb("small", [HEADS, 4, CH + 1])
    hd = sb("hd", [P, 3, SEQ])
    place[0] = rows_at
    t1 = sb("t1", [HEADS, CH, P])
    scanb = sb("scanb", [HEADS, 2, CH, P + P // 2])
    scanm = sb("scanm", [HEADS, 2, CH, P + P // 2])
    rrow = sb("rrow", [HEADS, CH, P])
    mrow = sb("mrow", [HEADS, CH, P])
    iwrow = sb("iwrow", [HEADS, CH, P])
    emrow = sb("emrow", [HEADS, CH, P])
    assert place[0] <= rows_at + 3 * HEADS * SEQ * 4
    wrow = rrow

    place[0] = arena
    aq = sb("aq", [P, DC, SEQ])
    ak = sb("ak", [P, DC, SEQ])
    av = sb("av", [P, CH, D])
    work_at = place[0]
    qf = sb("qf", [P, 2, SEQ])
    qsq = sb("qsq", [P, 2, SEQ])
    qrs = sb("qrs", [P, SEQ])
    place[0] = work_at
    sp = sb("sp", [P, 2, CH, SEQ])
    att = sb("att", [P, CH, SEQ])

    place[0] = arena
    qs = sb("qs", [P, 2, SEQ])
    sc = sb("sc", [P, 2, CH, NKEYS])
    sc2 = sb("sc2", [P, CH, NKEYS])
    v16 = sb("v16", [P, CH, PH, 2, TOPK])
    i16 = sb("i16", [P, CH, PH, 2, TOPK], U32)
    i16f = sb("i16f", [P, CH, PH, 2, TOPK])
    cand = sb("cand", [P, CH, TOPK * TOPK])
    cand2 = sb("cand2", [P, CH, TOPK * TOPK])
    topv = sb("topv", [P, CH, PH, TOPK])
    topi = sb("topi", [P, CH, PH, TOPK], U32)
    pos = sb("pos", [P, 2, CH, PH, TOPK], U32)
    posf = sb("posf", [P, 2, CH, PH, TOPK])
    pick = sb("pick", [P, PH, TOPK, TOPK])
    ex = sb("ex", [P, 3, CH, PH, TOPK])
    red = sb("red", [P, CH, PH])
    place[0] = arena
    stage = sb("stage", [P, 2, NKEYS, BATCH])
    exT = sb("exT", [P, 3, SEQ])
    one1 = sb("one1", [P, 2, 4, NKEYS])
    one2 = sb("one2", [P, 2, 4, NKEYS])

    place[0] = arena
    a_hi = sb("a_hi", [P, 2, GROUP, SEQ], F32R)
    a_lo = sb("a_lo", [P, 2, GROUP, SEQ], F32R)
    gates = sb("gates", [P, 2, NBATCH, UNIT, BATCH])
    gel = sb("gel", [P, 2, SEQ])
    prod = sb("prod", [P, SEQ])

    g_dram = [nc.dram_tensor(f"g_dram{l}", (NBATCH, P, NKEYS, BATCH), F32, kind="Internal").ap()
              for l in range(2)]

    bank = [ctx.enter_context(nc.psum_tensor(f"bank{i}", [P, SEQ], F32)) for i in range(RING)]
    misc = [ctx.enter_context(nc.psum_tensor(f"misc{i}", [P, SEQ], F32)) for i in range(4)]

    sems = {}

    def S(name):
        if name not in sems:
            sems[name] = ctx.enter_context(nc.semaphore(name))
        return sems[name]

    landed = [S(f"landed{i}") for i in range(RING)]
    split_hi, split_lo, tile_done = S("split_hi"), S("split_lo"), S("tile_done")
    emptied_sem = {"a": S("emptied_a"), "d": S("emptied_d")}

    def wait(eng, sem, value):
        if isinstance(value, int) and value <= 0:
            return
        eng.wait_ge(sem, value)

    def zbank(h, j):
        return (bank, misc)[h % 2][j]

    block = ctx.enter_context(nc.Block())

    @block.sync
    def _(sp_):
        def load(i, s):
            sp_.dma_start(raw[:, s, :], stream[ds(i * RING + s, 1), :, :].rearrange("a p n -> p (a n)")
                          ).then_inc(landed[s], 16)

        for s in range(RING):
            load(0, s)
        full = N_TILES // RING
        with sp_.Fori(1, full) as i:
            for s in range(RING):
                sp_.wait_ge(split_lo, i * RING + s - RING + 1)
                load(i, s)
        for t in range(full * RING, N_TILES):
            sp_.wait_ge(split_lo, t - RING + 1)
            load(full, t - full * RING)
        sp_.wait_ge(S("out_stored"), 16 * DC)

    @block.gpsimd
    def _(pool):
        def link(ins, n=[0]):
            n[0] += 1
            ins.then_inc(S("pool_link"), 1)
            pool.wait_ge(S("pool_link"), n[0])

        for t, v in ((ident, 0.0), (identb, 0.0), (ones, 1.0), (halfones, 1.0), (negtri, -1.0),
                     (negones, -1.0), (masked, MASKED), (causal, 1.0), (rowsel, 0.0)):
            last = pool.memset(t[:], v)
        link(last)
        for t in (ident, identb):
            pool.affine_select(out=t[:], in_=t[:], compare_op=ALU.not_equal, fill=1.0, base=0,
                               pattern=[[-1, P]], channel_multiplier=1)
        pool.affine_select(out=rowsel[:], in_=rowsel[:], compare_op=ALU.not_equal, fill=1.0, base=0,
                           pattern=[[-1, HEADS], [0, P]], channel_multiplier=1)
        for t in (negtri, masked):
            pool.affine_select(out=t[:], in_=t[:], compare_op=ALU.is_ge, fill=0.0, base=0,
                               pattern=[[-1, P]], channel_multiplier=1)
        pool.affine_select(out=causal[:], in_=causal[:], compare_op=ALU.is_ge, fill=0.0, base=0,
                           pattern=[[1, P]], channel_multiplier=-1)
        pool.affine_select(out=halfones[:, 0:HD], in_=halfones[:, 0:HD], compare_op=ALU.is_ge, fill=0.0,
                           base=HD - 1, pattern=[[0, HD]], channel_multiplier=-1)
        pool.affine_select(out=halfones[:, HD:], in_=halfones[:, HD:], compare_op=ALU.is_ge, fill=0.0,
                           base=-HD, pattern=[[0, HD]], channel_multiplier=1)
        pool.iota(iota[:], [[1, P]], base=0, channel_multiplier=0,
                  allow_small_or_imprecise_dtypes=True).then_inc(S("const_ready"), 1)

        def low(i, s):
            pool.wait_ge(split_hi, i * RING + s + 1)
            pool.tensor_tensor(w_lo[:, s, :], raw[:, s, :], w_hi[:, s, :].bitcast(F32),
                               ALU.subtract).then_inc(split_lo, 1)

        full = N_TILES // RING
        with pool.Fori(0, full) as i:
            for s in range(RING):
                low(i, s)
        for t in range(full * RING, N_TILES):
            low(full, t - full * RING)

    @block.scalar
    def _(act):
        def high(t, off=0):
            if t >= N_TILES:
                return
            s = t % RING
            act.wait_ge(landed[s], 16 * (t // RING + 1) + off * (16 // RING))
            wait(act, tile_done, t - RING + 1 + off)
            act.activation(w_hi[:, s, :], raw[:, s, :], ACT.Copy).then_inc(split_hi, 1)

        def link(ins, n=[0]):
            n[0] += 1
            ins.then_inc(S("act_link"), 1)
            act.wait_ge(S("act_link"), n[0])

        small_in = [(xT[:], x_t), (cvec[:], c.partition_broadcast(P)), (adab[:], ada_b), (gain[:], gains),
                    (gateb[:], gate_b), (convw[:], conv_w), (mnormc[:], mnorm), (keysT[:], keys),
                    (qkn[:], qk_norm)]
        act.dma_start(small_in[1][0], small_in[1][1]).then_inc(S("c_landed"), 16)
        for n in range(4):
            act.dma_start(ada_first[:, 4 * n:4 * n + 4, :],
                          ada[4 * n:4 * n + 4, :, :].rearrange("a p n -> p a n")
                          ).then_inc(S(f"ada_first{n}"), 16)
        for n, (dst, src) in enumerate(small_in):
            if n != 1:
                act.dma_start(dst, src).then_inc(S("x_landed" if n == 0 else "small_landed"), 16)

        def ada_load(n, off=0):
            wait(act, S("ada_used"), n - 1 + off)
            src = ada[ds(2 * DC + n + off, 1), :, :].rearrange("a p n -> p (a n)")
            act.dma_start(ada_w[:, n % 2, :], src).then_inc(S(f"ada{n % 2}"), 16)

        act.wait_ge(S("c_landed"), 16)
        act.activation(cvec[:], cvec[:], ACT.Silu).then_inc(S("silu"), 1)
        for t in range(LEAD):
            high(t)
        ada_load(0)
        ada_load(1)

        def norm(tag, x_ready, h_free):
            if x_ready:
                act.wait_ge(*x_ready)
            for k in range(DC):
                wait(act, S(tag + "_acc"), k - 1)
                act.activation(sq[:, k % 2, :], xT[:, k, :], ACT.Square).then_inc(S(tag + "_sq"), 1)
            act.wait_ge(S(tag + "_var"), 1)
            act.activation(rstd[:], rstd[:], ACT.Sqrt).then_inc(S(tag + "_std"), 1)
            for k in range(DC):
                act.wait_ge(S(tag + "_h"), k + 1)
                act.activation(h_hi[:, k, :], hw[:, k % 2, :], ACT.Copy).then_inc(S(tag + "_hi"), 1)

        norm("n0", (S("x_landed"), 16), None)

        for m in range(N_IN):
            t = IN0 + m
            high(t + LEAD)
            if m < 15:
                ada_load(2 * m + 2)
                ada_load(2 * m + 3)
            act.wait_ge(tile_done, t + 1)
            b = bank[t % RING]
            e = emptied_sem["a"]
            if m == 0:
                act.activation(li[:], b[0:HEADS, :].rearrange("p (c n) -> p c n", c=CH), ACT.Copy)
                act.activation(lf[:], b[32:32 + HEADS, :].rearrange("p (c n) -> p c n", c=CH), ACT.Copy
                               ).then_inc(e, 1)
                continue
            which, k = divmod(m - 1, 4)
            dst = (qT, kT, vT, oT, cbT, ccT, chT)[which]
            if which == 0:
                act.activation(dst[:, k, :], b[:], ACT.Copy, scale=float(P) ** -0.5).then_inc(e, 1)
            elif which == 3:
                act.activation(dst[:, k, :], b[:], ACT.Sigmoid).then_inc(e, 1)
            else:
                act.activation(dst[:, k, :], b[:], ACT.Copy).then_inc(e, 1)
        for k in range(HEADS):
            act.wait_ge(S("conv"), k + 1)
            act.activation(h_hi[:, HEADS + k, :], chT[:, k, :], ACT.Copy).then_inc(S("conv_hi"), 1)
        act.wait_ge(S("row_abs"), 1)
        link(act.activation(t1[:], t1[:], ACT.Exp, scale=-1.0))
        act.activation(t1[:], t1[:], ACT.Ln, bias=1.0).then_inc(S("row_ln"), 1)
        act.wait_ge(S("row_m"), 1)
        for k in range(CH):
            mp = small[:, 0, k:k + 1]
            act.activation(iwrow[:, k, :], mrow[:, k, :], ACT.Exp, scale=-1.0, bias=mp)
            act.activation(small[:, 3, k:k + 1], small[:, 1, k:k + 1], ACT.Exp, scale=-1.0, bias=mp)
        act.activation(emrow[:], emrow[:], ACT.Exp, scale=-1.0).then_inc(S("row_exp"), 1)
        act.wait_ge(S("r_tp"), 1)
        for k in range(CH):
            last = act.activation(wrow[:, k, :], rrow[:, k, :], ACT.Exp, bias=small[:, 2, k:k + 1])
        last.then_inc(S("row_w"), 1)
        for h in range(HEADS):
            act.wait_ge(S("v_tp"), h + 1)
            act.activation(v_nat[:, :, 0:P], misc[3][:].rearrange("p (c n) -> p c n", c=CH),
                           ACT.Copy).then_inc(S("v_nat"), 1)
            act.wait_ge(S("d_arg"), h + 1)
            act.activation(hd[:, 0, :], hd[:, 0, :], ACT.Exp, scale=-1.0).then_inc(S("d_exp"), 1)
            act.wait_ge(S("den"), h + 1)
            act.activation(hd[:, 2, :], misc[1][:], ACT.Abs).then_inc(S("den_abs"), 1)
            act.wait_ge(S("hm"), h + 1)
            act.activation(hd[:, 2, :], hd[:, 1, :], ACT.Square).then_inc(S("hm_sq"), 1)
            act.wait_ge(S("hm_var"), h + 1)
            act.activation(hd[:, 2, :], hd[:, 2, :], ACT.Sqrt).then_inc(S("hm_std"), 1)
            act.wait_ge(S("mix"), h + 1)
            act.activation(h_hi[:, h, :], hd[:, 0, :], ACT.Copy).then_inc(S("mix_hi"), 1)

        def projected_out(layer):
            for m in range(N_OUT):
                high(OUTP[layer] + m + LEAD)

        def peer(layer):
            L = str(layer)
            norm("f" + L, (emptied_sem["d"], emptied("d", OUTP[layer] + N_OUT - 1)), None)

            def scores_out(m):
                act.wait_ge(S("scores" + L), m + 1)
                wait(act, S("ranked" + L), m - 1)
                act.activation(sc[:, m % 2, :, :], misc[m % 2][:].rearrange("p (c n) -> p c n", c=CH),
                               ACT.Copy).then_inc(S("sc" + L), 1)

            for m in range(N_WQ):
                t = WQ[layer] + m
                high(t + LEAD)
                act.wait_ge(tile_done, t + 1)
                wait(act, S("scores" + L), m - 1)
                act.activation(qs[:, m % 2, :], bank[t % RING][:], ACT.Copy
                               ).then_inc(emptied_sem["a"], 1)
                if m:
                    scores_out(m - 1)
            scores_out(N_WQ - 1)
            act.wait_ge(S("gate_arg" + L), 1)
            act.activation(ex[:, 2, :, :], ex[:, 2, :, :], ACT.Exp).then_inc(S("gate_exp" + L), 1)
            for n in range(3):
                act.wait_ge(S("ex_tp" + L), n + 1)
                act.activation(exT[:, n, :], misc[n][:], ACT.Copy).then_inc(S("exT" + L), 1)
            link(act.activation(grant[:], ones[:, 0:1], ACT.Copy))
            act.activation(grant[:], ones[:, 0:1], ACT.Copy).then_inc(S("g_out" + L), 4)
            for s in range(2):
                act.wait_ge(S("g_out" + L), 4)
                act.wait_ge(S(f"stored{L}0"), 16) if s else None
                act.activation(grant[:], ones[:, 0:1], ACT.Copy).then_inc(S(f"stored{L}{s}"), 16)
            quads = BATCH // 4
            with act.Fori(0, NBATCH // 2) as i:
                for q in range(2 * quads):
                    s = q // quads
                    act.wait_ge(S("g_mm" + L), i * (2 * quads) + q + 3)
                    if q % quads == 0:
                        act.wait_ge(S(f"stored{L}{s}"), i * 16 + 16)
                    act.activation(stage[:, s, :, 4 * (q % quads):4 * (q % quads) + 4],
                                   misc[q % 4][:].rearrange("p (t e) -> p e t", t=4),
                                   ACT.Copy).then_inc(S("g_out" + L), 1)
                    if q % quads == quads - 1:
                        act.wait_ge(S("g_out" + L), i * (2 * quads) + q + 5)
                        act.dma_start(g_dram[layer][ds(i * 2 + s, 1)].rearrange("a p e t -> p (a e t)"),
                                      stage[:, s, :, :].rearrange("p e t -> p (e t)")
                                      ).then_inc(S(f"stored{L}{s}"), 16)
            for s in range(2):
                act.wait_ge(S(f"stored{L}{s}"), 16 * (NBATCH // 2) + 16)
            def load_gates(u, off=0):
                if not isinstance(off, int) or u >= 2:
                    act.wait_ge(S("acted" + L), UNIT * (u - 1 + off))
                act.dma_start(gates[:, u % 2, :, :, :],
                              g_dram[layer].rearrange("b p e t -> p b e t")[:, :, ds((u + off) * UNIT, UNIT), :]
                              ).then_inc(S(f"gates{L}{u % 2}"), 16)

            def u_tiles(t0, g, i=0, turn=0):
                for k in range(GROUP):
                    t = t0 + k
                    high(t + LEAD, 32 * i if turn else 0)
                    if k % UNIT == 0:
                        u = g * 2 + k // UNIT + 1
                        if turn or u < 2 * NGROUP:
                            load_gates(u, i * 4 if turn else 0)
                    act.wait_ge(tile_done, t + 1 + (32 * i if turn else 0))
                    n = g * GROUP + k
                    if turn or n >= 2:
                        act.wait_ge(S("acted" + L), n - 1 + (16 * i if turn else 0))
                    act.activation(gel[:, k % 2, :], bank[t % RING][:], ACT.Gelu
                                   ).then_inc(emptied_sem["a"], 1)

            def v_tiles(t0, first_ada, i=0, turn=0):
                for k in range(GROUP):
                    high(t0 + k + LEAD, 32 * i if turn else 0)
                    if layer == 0 and k in (0, 2, 4):
                        ada_load(first_ada + k // 2, 6 * i if turn else 0)

            t0 = DENSE[layer]
            load_gates(0)
            u_tiles(t0, 0)
            with act.Fori(0, (NGROUP - 2) // 2) as i:
                for half in range(2):
                    u_tiles(t0 + GROUP + 16 * half, 1 + half, i, 1)
                    v_tiles(t0 + 2 * GROUP + 16 * half, 4 * DC + 3 * half, i, 1)
            last = t0 + GROUP + 16 * (NGROUP - 2)
            u_tiles(last, NGROUP - 1)
            v_tiles(last + GROUP, 4 * DC + 42)
            v_tiles(last + 2 * GROUP, 4 * DC + 45)

        projected_out(0)
        peer(0)

        norm("n1", (emptied_sem["d"], emptied("d", QKV1 - 1)), None)

        def root(m):
            act.wait_ge(S("qk_var"), m + 1)
            act.activation(qrs[:], qrs[:], ACT.Sqrt).then_inc(S("qk_std"), 1)

        def v_out(k):
            act.wait_ge(S("av_tp"), k + 1)
            act.activation(av[:, :, k * P:(k + 1) * P], misc[k % 2][:].rearrange("p (c n) -> p c n", c=CH),
                           ACT.Copy).then_inc(S("av_out"), 1)

        for m in range(N_QKV):
            t = QKV1 + m
            high(t + LEAD)
            act.wait_ge(tile_done, t + 1)
            if m < 2 * DC:
                wait(act, S("qk_done"), m - 1)
                act.activation(qsq[:, m % 2, :], bank[t % RING][:], ACT.Square)
                act.activation(qf[:, m % 2, :], bank[t % RING][:], ACT.Copy
                               ).then_inc(emptied_sem["a"], 1)
            else:
                if m < 2 * DC + 2:
                    act.wait_ge(S("qk_done"), m - 1)
                wait(act, S("av_tp"), m - 2 * DC - 1)
                act.activation(qf[:, m % 2, :], bank[t % RING][:], ACT.Copy
                               ).then_inc(emptied_sem["a"], 1)
            if 1 <= m <= 2 * DC:
                root(m - 1)
            if m > 2 * DC:
                v_out(m - 2 * DC - 1)
        v_out(DC - 1)

        def sticks(h):
            for j in range(CH):
                act.wait_ge(S("z_abs"), CH * h + j + 1)
                zs = sp[:, h % 2, j, j * P:]
                act.activation(zs, zs, ACT.Exp, scale=-1.0).then_inc(S("z_exp"), 1)
                act.wait_ge(S("z_exp"), CH * h + j + 1)
                act.activation(zs, zs, ACT.Ln, bias=1.0).then_inc(S("z_ln"), 1)

        def weights(h):
            for j in range(CH):
                act.wait_ge(S("logw"), CH * h + j + 1)
                wait(act, S("att_out"), h)
                act.activation(att[:, j, j * P:], zbank(h, j)[:, j * P:], ACT.Exp).then_inc(S("att"), 1)

        def mixed(h):
            o = HD * (h % 2)
            act.wait_ge(S("att_out"), h + 1)
            act.activation(h_hi[o:o + HD, h // 2, :], zbank(h, 0)[o:o + HD, :], ACT.Copy
                           ).then_inc(S("o_hi"), 1)

        sticks(0)
        for h in range(SB_HEADS):
            if h + 1 < SB_HEADS:
                sticks(h + 1)
            weights(h)
            mixed(h)
        projected_out(1)
        peer(1)
        for m in range(DC):
            act.wait_ge(emptied_sem["d"], emptied("d", N_TILES - 1) - DC + m + 1)
            act.dma_start(out_t[:, m, :], xT[:, m, :]).then_inc(S("out_stored"), 16)

    @block.tensor
    def _(pe):
        def tile(t, hi, lo, off=0, loop=False, ready=None):
            b = bank[t % RING]
            pe.wait_ge(split_lo, t + 1 + off)
            if loop == "first":
                pe.wait_ge(emptied_sem["a"], loop_a + (off // 2))
                pe.wait_ge(emptied_sem["d"], emptied("d", t + 32 - RING) - 16 + off // 2)
            elif t >= RING:
                k = EVAC[t - RING]
                pe.wait_ge(emptied_sem[k], emptied(k, t - RING) + (off // 2 if loop else 0))
            for k in range(DC):
                if ready:
                    ready(k)
                wh = w_hi[:, t % RING, k * P:(k + 1) * P]
                wl = w_lo[:, t % RING, k * P:(k + 1) * P]
                pe.matmul(b[:], wh, hi(k), start=(k == 0), stop=False)
                pe.matmul(b[:], wh, lo(k), start=False, stop=False)
                mm = pe.matmul(b[:], wl, hi(k), start=False, stop=(k == DC - 1))
            mm.then_inc(tile_done, 1)

        loop_a = 0

        def h_tile(t, **kw):
            tile(t, lambda k: h_hi[:, k, :], lambda k: h_lo[:, k, :], **kw)

        def norm(tag):
            pe.wait_ge(S(tag + "_acc"), DC)
            pe.matmul(misc[0][:], ones[:], acc[:], start=True, stop=True).then_inc(S(tag + "_sum"), 1)

        pe.wait_ge(S("const_ready"), 1)
        norm("n0")
        for m in range(N_IN):
            h_tile(IN0 + m, ready=(lambda k: pe.wait_ge(S("n0_lo"), k + 1)) if m == 0 else None)

        pe.wait_ge(S("row_r"), 1)
        for k in range(CH):
            last = pe.transpose(misc[0][:, k * HEADS:(k + 1) * HEADS], rrow[:, k, :], ident[0:HEADS, 0:HEADS])
        last.then_inc(S("r_tp"), 1)
        pe.wait_ge(S("row_exp"), 1)
        for h in range(HEADS):
            last = pe.matmul(misc[2][:, h * CH:(h + 1) * CH], rowsel[:, h, :], small[:, 3, 0:CH],
                             start=True, stop=True)
        last.then_inc(S("decay_mm"), 1)
        pe.wait_ge(S("row_w"), 1)
        for k in range(CH):
            last = pe.transpose(misc[1][:, k * HEADS:(k + 1) * HEADS], wrow[:, k, :], ident[0:HEADS, 0:HEADS])
        last.then_inc(S("w_tp"), 1)
        pe.wait_ge(S("cols"), 3)
        for h in range(HEADS):
            wait(pe, S("hm"), h)
            for k in range(CH - 1):
                last = pe.transpose(misc[2][:, k * P:(k + 1) * P], kT[:, h, k * P:(k + 1) * P], ident[:])
            last.then_inc(S("k_tp"), 1)
            pe.matmul(misc[0][:], rowsel[:, h, :], mrow[:], start=True, stop=True).then_inc(S("m_mm"), 1)
            for k in range(CH):
                c_ = slice(k * P, (k + 1) * P)
                last = pe.matmul(misc[1][:, c_], kT[:, h, c_], qT[:, h, c_], start=True, stop=True)
            last.then_inc(S("qk_mm"), 1)
            wait(pe, S("hm_var"), h)
            for k in range(CH):
                last = pe.transpose(misc[3][:, k * P:(k + 1) * P], vT[:, h, k * P:(k + 1) * P], ident[:])
            last.then_inc(S("v_tp"), 1)
            pe.wait_ge(S("kw"), h + 1)
            pe.matmul(misc[2][:], rowsel[:, h, :], iwrow[:], start=True, stop=True).then_inc(S("iw_mm"), 1)
            pe.wait_ge(S("v_nat"), h + 1)
            pe.wait_ge(S("d_arg"), h + 1)
            for k in range(CH - 1):
                b = (misc[3], misc[3], misc[0])[k]
                o = (0, 2 * P, 0)[k]
                last = pe.matmul(b[:, o:o + 2 * P], k_nat[:, k, :], v_nat[:, k, :], start=True, stop=True)
            last.then_inc(S("state_mm"), 1)
            pe.wait_ge(S("pt"), h + 1)
            pe.wait_ge(S("qw"), h + 1)
            pe.wait_ge(S("state"), h + 1)
            for b, vn, st, done in ((misc[1], lambda k: ones[:], P, "den"),
                                    (misc[2], lambda k: v_nat[:, k, 0:P], 0, "num")):
                for k in range(CH):
                    c_ = slice(k * P, (k + 1) * P)
                    last = pe.matmul(b[:, c_], vn(k), hd[:, 0, c_], start=True, stop=(k == 0))
                    if k:
                        last = pe.matmul(b[:, c_], state[:, k - 1, st:st + P], hd[:, 1, c_],
                                         start=False, stop=True)
                last.then_inc(S(done), 1)
            pe.matmul(misc[0][:], rowsel[:, h, :], emrow[:], start=True, stop=True).then_inc(S("em_mm"), 1)
            pe.wait_ge(S("hm_sq"), h + 1)
            pe.matmul(misc[3][:], ones[:], hd[:, 2, :], start=True, stop=True).then_inc(S("hm_ss"), 1)

        def mixed_ready(k):
            if k < HEADS:
                pe.wait_ge(S("mix_lo"), k + 1)
            else:
                pe.wait_ge(S("conv_lo"), k - HEADS + 1)

        for m in range(N_OUT):
            h_tile(OUT0 + m, ready=mixed_ready if m == 0 else None)

        def peer(layer):
            nonlocal loop_a
            L = str(layer)
            norm("f" + L)

            def scores(m):
                pe.wait_ge(emptied_sem["a"], emptied("a", WQ[layer] + m))
                wait(pe, S("sc" + L), m - 1)
                for k in range(CH):
                    last = pe.matmul(misc[m % 2][:, k * P:(k + 1) * P], qs[:, m % 2, k * P:(k + 1) * P],
                                     keysT[:, layer, m % 2, :], start=True, stop=True)
                last.then_inc(S("scores" + L), 1)

            for m in range(N_WQ):
                h_tile(WQ[layer] + m, ready=(lambda k: pe.wait_ge(S(f"f{L}_lo"), k + 1)) if m == 0 else None)
                if m:
                    scores(m - 1)
            scores(N_WQ - 1)
            for n in range(3):
                pe.wait_ge(S("ex" + L), n + 1)
                for k in range(CH):
                    last = pe.transpose(misc[n][:, k * P:(k + 1) * P],
                                        ex[:, n, k, :, :].rearrange("p h k -> p (h k)"), ident[:])
                last.then_inc(S("ex_tp" + L), 1)
            pe.wait_ge(S("exT" + L), 3)
            quads = BATCH // 4
            with pe.Fori(0, SEQ // 16) as i:
                for q in range(4):
                    pe.wait_ge(S("one" + L), i * 4 + q + 1)
                    pe.wait_ge(S("g_out" + L), i * 4 + q + 1)
                    for u in range(4):
                        last = pe.matmul(misc[q][:, u * P:(u + 1) * P], one1[:, q % 2, u, :],
                                         one2[:, q % 2, u, :], start=True, stop=True)
                    last.then_inc(S("g_mm" + L), 1)

            def act_tile(t, par, **kw):
                tile(t, lambda k: a_hi[:, par, k, :], lambda k: a_lo[:, par, k, :], **kw)

            def v_tiles(t0, g, **kw):
                off = kw.get("off", 0)
                pe.wait_ge(S("acted" + L), GROUP * (g + 1) + (off // 2 if kw else 0))
                for k in range(GROUP):
                    act_tile(t0 + k, g % 2, **kw)

            t0 = DENSE[layer]
            for k in range(GROUP):
                h_tile(t0 + k)
            loop_a = emptied("a", t0 + GROUP - 1)
            with pe.Fori(0, (NGROUP - 2) // 2) as i:
                for half in range(2):
                    u0 = t0 + GROUP + 16 * half
                    for k in range(GROUP):
                        h_tile(u0 + k, off=i * 32, loop="first" if half == 0 and k < RING else True)
                    v_tiles(u0 + GROUP, half, off=i * 32, loop=True)
            last = t0 + GROUP + 16 * (NGROUP - 2)
            for k in range(GROUP):
                h_tile(last + k)
            v_tiles(last + GROUP, NGROUP - 2)
            v_tiles(last + 2 * GROUP, NGROUP - 1)

        peer(0)

        norm("n1")

        def square_sums(m):
            pe.wait_ge(emptied_sem["a"], emptied("a", QKV1 + m))
            wait(pe, S("qk_var"), m - 1)
            pe.matmul(misc[2 + m % 2][:], halfones[:], qsq[:, m % 2, :], start=True, stop=True
                      ).then_inc(S("qk_ss"), 1)

        def turn_v(k):
            pe.wait_ge(emptied_sem["a"], emptied("a", QKV1 + 2 * DC + k))
            wait(pe, S("av_out"), k - 1)
            for j in range(CH):
                last = pe.transpose(misc[k % 2][:, j * P:(j + 1) * P], qf[:, k % 2, j * P:(j + 1) * P],
                                    ident[:])
            last.then_inc(S("av_tp"), 1)

        for m in range(N_QKV):
            h_tile(QKV1 + m, ready=(lambda k: pe.wait_ge(S("n1_lo"), k + 1)) if m == 0 else None)
            if 1 <= m <= 2 * DC:
                square_sums(m - 1)
            if m > 2 * DC:
                turn_v(m - 2 * DC - 1)
        turn_v(DC - 1)
        pe.wait_ge(S("qk_done"), 2 * DC)
        pe.wait_ge(S("av_out"), DC)

        def logits(h):
            o, m = HD * (h % 2), h // 2
            if h >= 2:
                pe.wait_ge(S("o_hi"), h - 1)
                pe.wait_ge(S("o_lo"), h - 1)
            for j in range(CH):
                b = zbank(h, j)
                pe.matmul(b[:, j * P:], ak[o:o + HD, m, j * P:(j + 1) * P], aq[o:o + HD, m, j * P:],
                          start=True, stop=False, skip_group_check=True)
                pe.matmul(b[:, j * P:(j + 1) * P], identb[:], masked[:], start=False, stop=(True),
                          skip_group_check=True).then_inc(S("z"), 1)

        def log_weights(h):
            for j in range(CH):
                if j == 0:
                    pe.wait_ge(S("sp"), CH * (h + 1))
                b = zbank(h, j)
                last = pe.matmul(b[:, j * P:], negtri[:], sp[:, h % 2, j, j * P:], start=False, stop=True,
                                 skip_group_check=True)
                for n in range(j + 1, CH):
                    last = pe.matmul(b[:, n * P:], negones[:], sp[:, h % 2, n, n * P:], start=False,
                                     stop=True, skip_group_check=True)
                last.then_inc(S("logw"), 1)

        def weighted(h):
            o = HD * (h % 2)
            for j in range(CH):
                pe.wait_ge(S("att"), CH * h + j + 1)
                last = pe.matmul(zbank(h, 0)[o:o + HD, j * P:], av[:, j, h * HD:(h + 1) * HD],
                                 att[:, j, j * P:], start=(j == 0), stop=(j == CH - 1), skip_group_check=True)
            last.then_inc(S("att_out"), 1)

        logits(0)
        for h in range(SB_HEADS):
            if h + 1 < SB_HEADS:
                logits(h + 1)
            log_weights(h)
            weighted(h)
        pe.wait_ge(S("o_lo"), SB_HEADS)
        for m in range(N_OUT):
            h_tile(OUT1 + m)
        peer(1)

    @block.vector
    def _(dve):
        links = [0]

        def link(ins):
            links[0] += 1
            ins.then_inc(S("dve_link"), 1)
            dve.wait_ge(S("dve_link"), links[0])

        def ada_dot(n, dst, off=0):
            s = n % 2
            dve.wait_ge(S(f"ada{s}"), 16 * (n // 2 + 1) + (off * 8))
            dve.tensor_tensor_reduce(ada_w[:, s, :], ada_w[:, s, :], cvec[:], 1.0, 0.0, ALU.mult, ALU.add,
                                     dst).then_inc(S("ada_used"), 1)

        def columns(n, l, part):
            dve.scalar_tensor_tensor(out=scol[:, n, :], in0=mod[:, l, part + DC:part + 2 * DC], scalar=1.0,
                                     in1=gain[:, n, :], op0=ALU.add, op1=ALU.mult)

        def norm(tag, n, l, part, h_free=None):
            for k in range(DC):
                dve.wait_ge(S(tag + "_sq"), k + 1)
                if k == 0:
                    dve.tensor_copy(acc[:], sq[:, 0, :]).then_inc(S(tag + "_acc"), 1)
                else:
                    dve.wait_ge(S(tag + "_acc"), k)
                    dve.tensor_tensor(acc[:], acc[:], sq[:, k % 2, :], ALU.add).then_inc(S(tag + "_acc"), 1)
            dve.wait_ge(S(tag + "_sum"), 1)
            dve.tensor_scalar(rstd[:], misc[0][:], 1.0 / D, EPS, ALU.mult, ALU.add).then_inc(S(tag + "_var"), 1)
            dve.wait_ge(S(tag + "_std"), 1)
            link(dve.reciprocal(rstd[:], rstd[:]))

            def low(k):
                dve.wait_ge(S(tag + "_hi"), k + 1)
                dve.tensor_tensor(h_lo[:, k, :], hw[:, k % 2, :], h_hi[:, k, :].bitcast(F32),
                                  ALU.subtract).then_inc(S(tag + "_lo"), 1)

            for k in range(DC + 1):
                if k < DC:
                    wait(dve, S(tag + "_lo"), k - 1)
                    link(dve.tensor_tensor(hw[:, k % 2, :], xT[:, k, :], rstd[:], ALU.mult))
                    dve.tensor_scalar(hw[:, k % 2, :], hw[:, k % 2, :], scol[:, n, k:k + 1],
                                      mod[:, l, part + k:part + k + 1], ALU.mult, ALU.add
                                      ).then_inc(S(tag + "_h"), 1)
                if k:
                    low(k - 1)

        def x_update(t, m, n, off=0):
            dve.wait_ge(tile_done, t + 1 + off)
            if emptied("d", t) > DC:
                dve.wait_ge(emptied_sem["d"], emptied("d", t) - DC + (off // 2))
            dve.scalar_tensor_tensor(out=xT[:, m, :], in0=bank[t % RING][:], scalar=g1p[:, n, m:m + 1],
                                     in1=xT[:, m, :], op0=ALU.mult, op1=ALU.add
                                     ).then_inc(emptied_sem["d"], 1)

        dve.wait_ge(S("silu"), 1)
        for n in range(2 * DC):
            if n % 4 == 0:
                dve.wait_ge(S(f"ada_first{n // 4}"), 16)
            last = dve.tensor_tensor_reduce(ada_first[:, n, :], ada_first[:, n, :], cvec[:], 1.0, 0.0,
                                            ALU.mult, ALU.add, mod[:, 0, n:n + 1])
        link(last)
        dve.wait_ge(S("small_landed"), 16 * 7)
        link(dve.tensor_tensor(mod[:, 0, 0:2 * DC], mod[:, 0, 0:2 * DC], adab[:, 0, 0:2 * DC], ALU.add))
        columns(0, 0, 0)
        dve.wait_ge(S("x_landed"), 16)
        link(dve.tensor_scalar(qkn[:, 0:1], qkn[:, 0:1], float(HD) ** -0.5, None, ALU.mult))
        norm("n0", 0, 0, 0)
        for n in range(4 * DC):
            ada_dot(n, mod[:, 0, 2 * DC + n:2 * DC + n + 1])
        dve.wait_ge(S("ada_used"), 4 * DC)
        link(dve.tensor_tensor(mod[:, 0, 2 * DC:], mod[:, 0, 2 * DC:], adab[:, 0, 2 * DC:], ALU.add))
        dve.tensor_scalar(g1p[:, 0, :], mod[:, 0, 2 * DC:3 * DC], 1.0, None, ALU.add)
        dve.tensor_scalar(g1p[:, 1, :], mod[:, 0, 5 * DC:6 * DC], 1.0, None, ALU.add)
        columns(1, 0, 3 * DC)

        dve.wait_ge(emptied_sem["a"], N_IN)
        for k in range(HEADS):
            u, y = ccT[:, k, :], chT[:, k, :]
            link(dve.tensor_tensor(u, ccT[:, k, :], chT[:, k, :], ALU.mult))
            link(dve.tensor_scalar(y, u, convw[:, k, 2:3], None, ALU.mult))
            for n in (1, 2):
                link(dve.scalar_tensor_tensor(out=chT[:, k, n:], in0=ccT[:, k, 0:SEQ - n],
                                              scalar=convw[:, k, 2 - n:3 - n], in1=chT[:, k, n:],
                                              op0=ALU.mult, op1=ALU.add))
            dve.tensor_tensor(y, y, cbT[:, k, :], ALU.mult).then_inc(S("conv"), 1)
            dve.wait_ge(S("conv_hi"), k + 1)
            dve.tensor_tensor(h_lo[:, HEADS + k, :], y, h_hi[:, HEADS + k, :].bitcast(F32), ALU.subtract
                              ).then_inc(S("conv_lo"), 1)

        dve.wait_ge(S("conv_lo"), HEADS)
        dve.memset(v_nat[:, :, P:], 1.0)
        dve.tensor_scalar(li[:], li[:], gateb[:, 0:1], None, ALU.add)
        link(dve.tensor_scalar(lf[:], lf[:], gateb[:, 1:2], None, ALU.add))
        dve.tensor_scalar(t1[:].bitcast(U32), lf[:].bitcast(U32), NO_SIGN, None, ALU.bitwise_and
                          ).then_inc(S("row_abs"), 1)
        H = P // 2
        dve.memset(scanb[:, :, :, 0:H], 0.0)
        dve.memset(scanm[:, :, :, 0:H], LOWEST)
        link(dve.memset(small[:], 0.0))
        dve.wait_ge(S("row_ln"), 1)
        link(dve.scalar_tensor_tensor(out=scanb[:, 0, :, H:], in0=lf[:], scalar=0.0, in1=t1[:],
                                      op0=ALU.min, op1=ALU.subtract))

        def scan(buf, op):
            for n in range(7):
                a, b, w = n % 2, (n + 1) % 2, 1 << n
                link(dve.tensor_tensor(buf[:, b, :, H:], buf[:, a, :, H:], buf[:, a, :, H - w:H + P - w], op))

        scan(scanb, ALU.add)
        bsum = scanb[:, 1, :, H:]
        link(dve.tensor_tensor(rrow[:], li[:], bsum, ALU.subtract))
        dve.tensor_copy(scanm[:, 0, :, H:], rrow[:]).then_inc(S("row_r"), 1)
        dve.wait_ge(S("row_r"), 1)
        scan(scanm, ALU.max)
        cm = scanm[:, 1, :, H:]
        for k in range(CH):
            link(dve.tensor_tensor(small[:, 1, k:k + 1], small[:, 0, k:k + 1], cm[:, k, P - 1:P], ALU.max))
            link(dve.tensor_tensor(small[:, 0, k + 1:k + 2], small[:, 1, k:k + 1], bsum[:, k, P - 1:P], ALU.add))
        for k in range(CH):
            last = dve.tensor_scalar(mrow[:, k, :], cm[:, k, :], small[:, 0, k:k + 1], None, ALU.max)
        link(last)
        dve.tensor_scalar(small[:, 2, 0:CH], small[:, 1, 0:CH], -1.0, None, ALU.mult)
        dve.tensor_tensor(emrow[:], mrow[:], bsum, ALU.add).then_inc(S("row_m"), 1)
        dve.wait_ge(S("r_tp"), 1)
        dve.tensor_copy(gcols[:, 0, :, :], misc[0][:, 0:CH * HEADS].rearrange("p (c h) -> p c h", c=CH)
                        ).then_inc(S("cols"), 1)
        dve.wait_ge(S("decay_mm"), 1)
        dve.tensor_copy(decay_b[:], misc[2][:, 0:CH * HEADS].rearrange("p (h c) -> p h c", c=CH)
                        ).then_inc(S("cols"), 1)
        dve.wait_ge(S("w_tp"), 1)
        dve.tensor_copy(gcols[:, 1, :, :], misc[1][:, 0:CH * HEADS].rearrange("p (c h) -> p c h", c=CH)
                        ).then_inc(S("cols"), 1)
        dve.wait_ge(S("cols"), 3)

        def by_chunk(ap):
            return ap.rearrange("p (c n) -> p c n", c=CH)

        w0, w1, w2 = (hd[:, n, :] for n in range(3))
        for h in range(HEADS):
            dve.wait_ge(S("k_tp"), h + 1)
            for k in range(CH - 1):
                last = dve.tensor_scalar(k_nat[:, k, :], misc[2][:, k * P:(k + 1) * P],
                                         gcols[:, 1, k, h:h + 1], None, ALU.mult)
            last.then_inc(S("kw"), 1)
            dve.wait_ge(S("m_mm"), h + 1)
            wait(dve, S("mix_lo"), h)
            link(dve.tensor_tensor(by_chunk(w0), by_chunk(misc[0][:]),
                                   gcols[:, 0, :, h:h + 1].to_broadcast([P, CH, P]), ALU.subtract))
            dve.tensor_scalar(w0, w0, 0.0, None, ALU.max).then_inc(S("d_arg"), 1)
            dve.wait_ge(S("iw_mm"), h + 1)
            dve.tensor_tensor(w1, qT[:, h, :], misc[2][:], ALU.mult).then_inc(S("qw"), 1)
            dve.wait_ge(S("state_mm"), h + 1)
            link(dve.tensor_copy(state[:, 0, :], misc[3][:, 0:2 * P]))
            for k in range(1, CH - 1):
                src = misc[3][:, 2 * P:] if k == 1 else misc[0][:, 0:2 * P]
                last = dve.scalar_tensor_tensor(out=state[:, k, :], in0=state[:, k - 1, :],
                                                scalar=decay_b[:, h, k:k + 1], in1=src, op0=ALU.mult, op1=ALU.add)
                if k < CH - 2:
                    link(last)
            last.then_inc(S("state"), 1)
            dve.wait_ge(S("d_exp"), h + 1)
            dve.wait_ge(S("qk_mm"), h + 1)
            link(dve.tensor_tensor(w0, w0, misc[1][:], ALU.mult))
            dve.tensor_tensor(by_chunk(w0), by_chunk(w0), causal[:].unsqueeze(1).to_broadcast([P, CH, P]),
                              ALU.mult).then_inc(S("pt"), 1)
            dve.wait_ge(S("den_abs"), h + 1)
            dve.wait_ge(S("em_mm"), h + 1)
            link(dve.tensor_tensor(w2, w2, misc[0][:], ALU.max))
            link(dve.reciprocal(w2, w2))
            dve.wait_ge(S("num"), h + 1)
            dve.tensor_tensor(w1, misc[2][:], w2, ALU.mult).then_inc(S("hm"), 1)
            dve.wait_ge(S("hm_ss"), h + 1)
            dve.tensor_scalar(w2, misc[3][:], 1.0 / P, EPS, ALU.mult, ALU.add).then_inc(S("hm_var"), 1)
            dve.wait_ge(S("hm_std"), h + 1)
            link(dve.reciprocal(w2, w2))
            link(dve.tensor_tensor(w1, w1, w2, ALU.mult))
            dve.scalar_tensor_tensor(out=w0, in0=w1, scalar=mnormc[:, h:h + 1], in1=oT[:, h, :],
                                     op0=ALU.mult, op1=ALU.mult).then_inc(S("mix"), 1)
            dve.wait_ge(S("mix_hi"), h + 1)
            dve.tensor_tensor(h_lo[:, h, :], w0, h_hi[:, h, :].bitcast(F32), ALU.subtract
                              ).then_inc(S("mix_lo"), 1)

        def output(layer):
            for m in range(N_OUT):
                x_update(OUTP[layer] + m, m, 2 * layer)

        def peer(layer):
            L = str(layer)
            norm("f" + L, 2 * layer + 1, layer, 3 * DC)

            def step(instructions):
                for ins in instructions:
                    last = ins()
                link(last)

            def top16(values, spare, v, i):
                r = range(CH)
                step([lambda c=c: dve.max(v(c)[:, 0:8], values(c)) for c in r])
                step([lambda c=c: dve.max_index(i(c)[:, 0:8], v(c)[:, 0:8], values(c)) for c in r] +
                     [lambda c=c: dve.match_replace(spare(c), v(c)[:, 0:8], values(c), LOWEST) for c in r])
                step([lambda c=c: dve.max(v(c)[:, 8:16], spare(c)) for c in r])
                return [lambda c=c: dve.max_index(i(c)[:, 8:16], v(c)[:, 8:16], spare(c)) for c in r]

            def rank(m):
                h, half = m // 2, m % 2
                dve.wait_ge(S("sc" + L), m + 1)
                for ins in top16(lambda c: sc[:, m % 2, c, :], lambda c: sc2[:, c, :],
                                 lambda c: v16[:, c, h, half, :], lambda c: i16[:, c, h, half, :]):
                    last = ins()
                last.then_inc(S("ranked" + L), 1)
                dve.wait_ge(S("ranked" + L), m + 1)

            def choose(h):
                link(dve.tensor_tensor(
                    cand[:].rearrange("p c (a b) -> p c a b", a=TOPK),
                    v16[:, :, h, 0, :].unsqueeze(3).to_broadcast([P, CH, TOPK, TOPK]),
                    v16[:, :, h, 1, :].unsqueeze(2).to_broadcast([P, CH, TOPK, TOPK]), ALU.add))
                step(top16(lambda c: cand[:, c, :], lambda c: cand2[:, c, :],
                           lambda c: topv[:, c, h, :], lambda c: topi[:, c, h, :]))

            for m in range(N_WQ):
                rank(m)
                if m % 2:
                    choose(m // 2)
            dve.tensor_tensor(ex[:, 2, :, :, :], topv[:], topv[:, :, :, 0:1].to_broadcast([P, CH, PH, TOPK]),
                              ALU.subtract).then_inc(S("gate_arg" + L), 1)
            dve.tensor_scalar(pos[:, 0], topi[:], 4, None, ALU.logical_shift_right)
            link(dve.tensor_scalar(pos[:, 1], topi[:], TOPK - 1, None, ALU.bitwise_and))
            dve.tensor_copy(posf[:], pos[:])
            link(dve.tensor_copy(i16f[:], i16[:]))
            for half in range(2):
                for c_ in range(CH):
                    where = posf[:, half, c_, :, :].unsqueeze(3).to_broadcast([P, PH, TOPK, TOPK])
                    index = i16f[:, c_, :, half, :].unsqueeze(2).to_broadcast([P, PH, TOPK, TOPK])
                    sixteen = iota[:, 0:TOPK].unsqueeze(1).unsqueeze(1).to_broadcast([P, PH, TOPK, TOPK])
                    link(dve.tensor_tensor(pick[:], where, sixteen, ALU.is_equal))
                    link(dve.tensor_tensor(pick[:], pick[:], index, ALU.mult))
                    last = dve.tensor_reduce(ex[:, half, c_, :, :], pick[:], AX_X, ALU.add)
                    if c_ < CH - 1:
                        link(last)
                last.then_inc(S("ex" + L), 1)
                dve.wait_ge(S("ex" + L), half + 1)
            dve.wait_ge(S("gate_exp" + L), 1)
            link(dve.tensor_reduce(red[:], ex[:, 2, :, :, :], AX_X, ALU.add))
            link(dve.reciprocal(red[:], red[:]))
            dve.tensor_tensor(ex[:, 2, :, :, :], ex[:, 2, :, :, :],
                              red[:].unsqueeze(3).to_broadcast([P, CH, PH, TOPK]), ALU.mult
                              ).then_inc(S("ex" + L), 1)
            dve.wait_ge(S("exT" + L), 3)
            dve.memset(one1[:, 0, 0, :], 0.0).then_inc(S("g_mm" + L), 2)
            with dve.Fori(0, SEQ // 16) as i:
                for q in range(4):
                    dve.wait_ge(S("g_mm" + L), i * 4 + q + 1)
                    for u in range(4):
                        tok = ds(i * 16 + 4 * q + u, 1)
                        dve.tensor_scalar(one1[:, q % 2, u, :], iota[:], exT[:, 0, tok], None, ALU.is_equal)
                        last = dve.tensor_scalar(one2[:, q % 2, u, :], iota[:], exT[:, 1, tok],
                                                 exT[:, 2, tok], ALU.is_equal, ALU.mult)
                    last.then_inc(S("one" + L), 1)

            def u_tiles(t0, g, i=0, turn=0):
                for k in range(GROUP):
                    t = t0 + k
                    o16 = 16 * i if turn else 0
                    u = g * 2 + k // UNIT
                    if k % UNIT == 0:
                        dve.wait_ge(S(f"gates{L}{u % 2}"), 16 * (u // 2 + 1) + (32 * i if turn else 0))
                    dve.wait_ge(emptied_sem["a"], emptied("a", t) + o16)
                    par = g % 2
                    link3(dve.tensor_tensor(prod[:].rearrange("p (b t) -> p b t", b=NBATCH),
                                            gel[:, k % 2, :].rearrange("p (b t) -> p b t", b=NBATCH),
                                            gates[:, u % 2, :, k % UNIT, :], ALU.mult), g, k, i, turn, 0)
                    link3(dve.tensor_copy(a_hi[:, par, k, :], prod[:]), g, k, i, turn, 1)
                    dve.tensor_tensor(a_lo[:, par, k, :], prod[:], a_hi[:, par, k, :].bitcast(F32),
                                      ALU.subtract).then_inc(S("acted" + L), 1)
                    dve.wait_ge(S("acted" + L), g * GROUP + k + 1 + o16)

            def link3(ins, g, k, i, turn, n):
                ins.then_inc(S("product" + L), 1)
                dve.wait_ge(S("product" + L), 2 * (g * GROUP + k) + n + 1 + (32 * i if turn else 0))

            def v_tiles(t0, first_ada, i=0, turn=0):
                for k in range(GROUP):
                    x_update(t0 + k, k, 2 * layer + 1, i * 32 if turn else 0)
                    if layer == 0 and k in (1, 3, 5):
                        n = first_ada + k // 2
                        off = 6 * i if turn else 0
                        ada_dot(n, adacol[:, n % 2:n % 2 + 1], off)
                        dve.wait_ge(S("ada_used"), n + 1 + off)
                        dve.tensor_copy(mod[:, 1, ds(n - 4 * DC + off, 1)], adacol[:, n % 2:n % 2 + 1])

            t0 = DENSE[layer]
            u_tiles(t0, 0)
            with dve.Fori(0, (NGROUP - 2) // 2) as i:
                for half in range(2):
                    u_tiles(t0 + GROUP + 16 * half, 1 + half, i, 1)
                    v_tiles(t0 + 2 * GROUP + 16 * half, 4 * DC + 3 * half, i, 1)
            last = t0 + GROUP + 16 * (NGROUP - 2)
            u_tiles(last, NGROUP - 1)
            v_tiles(last + GROUP, 4 * DC + 42)
            v_tiles(last + 2 * GROUP, 4 * DC + 45)

        output(0)
        peer(0)

        link(dve.tensor_copy(adacol[:, 0:1], adacol[:, 1:2]))
        link(dve.tensor_tensor(mod[:, 1, :], mod[:, 1, :], adab[:, 1, :], ALU.add))
        columns(2, 1, 0)
        columns(3, 1, 3 * DC)
        dve.tensor_scalar(g1p[:, 2, :], mod[:, 1, 2 * DC:3 * DC], 1.0, None, ALU.add)
        link(dve.tensor_scalar(g1p[:, 3, :], mod[:, 1, 5 * DC:6 * DC], 1.0, None, ALU.add))
        norm("n1", 2, 1, 0)
        for m in range(2 * DC):
            dve.wait_ge(S("qk_ss"), m + 1)
            dve.tensor_scalar(qrs[:], misc[2 + m % 2][:], 1.0 / HD, EPS, ALU.mult, ALU.add
                              ).then_inc(S("qk_var"), 1)
            dve.wait_ge(S("qk_std"), m + 1)
            link(dve.reciprocal(qrs[:], qrs[:]))
            which, k = divmod(m, DC)
            dve.scalar_tensor_tensor(out=(aq, ak)[which][:, k, :], in0=qf[:, m % 2, :],
                                     scalar=qkn[:, which:which + 1], in1=qrs[:], op0=ALU.mult, op1=ALU.mult
                                     ).then_inc(S("qk_done"), 1)
            dve.wait_ge(S("qk_done"), m + 1)

        def sticks(h):
            if h >= 2:
                dve.wait_ge(S("logw"), CH * (h - 1))
            for j in range(CH):
                dve.wait_ge(S("z"), CH * h + j + 1)
                dve.tensor_scalar(sp[:, h % 2, j, j * P:].bitcast(U32), zbank(h, j)[:, j * P:].bitcast(U32),
                                  NO_SIGN, None, ALU.bitwise_and).then_inc(S("z_abs"), 1)
            for j in range(CH):
                dve.wait_ge(S("z_ln"), CH * h + j + 1)
                dve.scalar_tensor_tensor(out=sp[:, h % 2, j, j * P:], in0=zbank(h, j)[:, j * P:], scalar=0.0,
                                         in1=sp[:, h % 2, j, j * P:], op0=ALU.max, op1=ALU.add
                                         ).then_inc(S("sp"), 1)

        sticks(0)
        for h in range(SB_HEADS):
            if h + 1 < SB_HEADS:
                sticks(h + 1)
            o = HD * (h % 2)
            dve.wait_ge(S("o_hi"), h + 1)
            dve.tensor_tensor(h_lo[o:o + HD, h // 2, :], zbank(h, 0)[o:o + HD, :],
                              h_hi[o:o + HD, h // 2, :].bitcast(F32), ALU.subtract).then_inc(S("o_lo"), 1)
        output(1)
        peer(1)

    ctx.close()


def kernel(**inputs):
    import numpy as np
    import concourse.bacc as bacc
    from concourse.bass_utils import run_bass_kernel_spmd as run

    a = {k: np.asarray(v) for k, v in inputs.items()}

    def tiles(w):
        return w.reshape(DC, P, -1, P).transpose(2, 1, 0, 3).reshape(-1, P, D)

    def expert_tiles(u, v):
        ut = u.reshape(P, NKEYS, DC, P).transpose(1, 3, 2, 0).reshape(NGROUP, GROUP, P, D)
        vt = v.reshape(P, NGROUP, GROUP, DC, P).transpose(1, 3, 0, 2, 4).reshape(NGROUP, DC, P, D)
        order = [ut[0]]
        for g in range(1, NGROUP):
            order += [ut[g], vt[g - 1]]
        return order + [vt[NGROUP - 1]]

    def col(v, n=D):
        return v.reshape(n // P, P).T

    w_in = a["l0_w_in"]
    W = HEADS * P
    gate_tile = np.zeros((D, P), w_in.dtype)
    gate_tile[:, 0:HEADS] = w_in[:, 4 * W:4 * W + HEADS]
    gate_tile[:, 32:32 + HEADS] = w_in[:, 4 * W + HEADS:4 * W + 2 * HEADS]
    stream = np.concatenate(
        [tiles(gate_tile), tiles(w_in[:, 0:4 * W]), tiles(w_in[:, 4 * W + 2 * HEADS:]), tiles(a["l0_w_out"]),
         tiles(a["l0_peer_wq"])] + expert_tiles(a["l0_peer_u"], a["l0_peer_v"]) +
        [tiles(a["l1_w_qkv"]), tiles(a["l1_w_out"]), tiles(a["l1_peer_wq"])] +
        expert_tiles(a["l1_peer_u"], a["l1_peer_v"]))
    data = {
        "stream": stream,
        "x_t": a["x"].reshape(SEQ, DC, P).transpose(2, 1, 0),
        "c": a["c"].reshape(D),
        "ada": np.concatenate([a[f"l{l}_ada_w"].T.reshape(ADA, P, D) for l in range(2)]),
        "ada_b": np.stack([col(a[f"l{l}_ada_b"], ADA * P) for l in range(2)], 1),
        "gains": np.stack([col(a[n]) for n in ("l0_norm_mix", "l0_norm_ffn", "l1_norm_mix", "l1_norm_ffn")], 1),
        "gate_b": np.stack([a["l0_b_igate"], a["l0_b_fgate"]], 1),
        "conv_w": a["l0_conv_w"].reshape(3, HEADS, P).transpose(2, 1, 0),
        "mnorm": col(a["l0_mlstm_norm"], W),
        "keys": np.stack([np.stack([a[f"l{l}_peer_k{n}"].T for n in (1, 2)], 1) for l in range(2)], 1),
        "qk_norm": np.stack([np.concatenate([a[n], a[n]]) for n in ("l1_q_norm", "l1_k_norm")], 1),
    }
    data = {k: np.ascontiguousarray(v) for k, v in data.items()}
    nc = bacc.Bacc("TRN2", target_bir_lowering=False, num_devices=1)
    args = [nc.dram_tensor(k + "_dram", v.shape, F32, kind="ExternalInput").ap() for k, v in data.items()]
    out_t = nc.dram_tensor("out_dram", (P, DC, SEQ), F32, kind="ExternalOutput").ap()
    build(nc, *args, out_t)
    r = run(nc, [{k + "_dram": v for k, v in data.items()}], core_ids=[0])
    return r.results[0]["out_dram"].transpose(2, 1, 0).reshape(1, SEQ, D)
```

```python
from contextlib import ExitStack

import concourse.bass as bass
from concourse import mybir

F32 = mybir.dt.float32
F32R = mybir.dt.float32r
BF16 = mybir.dt.bfloat16
U32 = mybir.dt.uint32
ALU = mybir.AluOpType
ACT = mybir.ActivationFunctionType
AX_X = mybir.AxisListType.X
ds = bass.ds

P = 128
SEQ = 512
D = 1024
DC = D // P
EPS = 1e-6
CH = SEQ // P
HEADS = 4
SB_HEADS = 16
HD = D // SB_HEADS
PH = 8
TOPK = 16
NKEYS = 128
GROUP = 8
NGROUP = NKEYS // GROUP
V_TURNS = (NGROUP - 4) // 2
UNIT = 2
U_EARLY, U_GATES = 40, 64
BATCH = 64
NBATCH = SEQ // BATCH
LOWEST = -3.0e38
MASKED = -1.0e30
HEADS_FROM = 13
ADA_FROM = 11
NO_SIGN = 0x7FFFFFFF

N_IN = 29
N_OUT = DC
N_WQ = 2 * PH
N_DENSE = 2 * NKEYS
N_QKV = 3 * DC
IN0 = 0
OUT0 = IN0 + N_IN
WQ0 = OUT0 + N_OUT
DENSE0 = WQ0 + N_WQ
QKV1 = DENSE0 + N_DENSE
OUT1 = QKV1 + N_QKV
WQ1 = OUT1 + N_OUT
DENSE1 = WQ1 + N_WQ
N_TILES = DENSE1 + N_DENSE
WQ = (WQ0, WQ1)
DENSE = (DENSE0, DENSE1)
OUTP = (OUT0, OUT1)
RING = 4
LEAD = 3
ADA = 6 * DC


def evacuators():
    dense = "a" * NKEYS + "d" * NKEYS
    layer = "d" * N_OUT + "a" * N_WQ + dense
    return "a" * N_IN + layer + "a" * N_QKV + layer


EVAC = evacuators()
assert len(EVAC) == N_TILES


def emptied(kind, t):
    return EVAC[:t + 1].count(kind)


def build(nc, stream, x_t, c, ada, ada_b, gains, gate_b, conv_w, mnorm, keys, qk_norm, out_t):
    ctx = ExitStack()
    base = -(-nc.sbuf_base // 64) * 64
    limit = nc.sbuf_usable_end
    place = [base]

    def sb(name, shape, dt=F32):
        size = mybir.dt.size(dt)
        for n in shape[1:]:
            size *= n
        t = nc.alloc_sbuf_tensor_at(name, shape, dt, offset=place[0])
        place[0] += -(-size // 64) * 64
        assert place[0] <= limit, (name, place[0], limit)
        return t

    ident = sb("ident", [P, P])
    identb = sb("identb", [P, P], BF16)
    ones = sb("ones", [P, P])
    halfones = sb("halfones", [P, P])
    negtri = sb("negtri", [P, P])
    masked = sb("masked", [P, P], BF16)
    causal = sb("causal", [P, P])
    rowsel = sb("rowsel", [HEADS, HEADS, P])
    iota = sb("iota", [P, P])
    iotab = sb("iotab", [P, P], BF16)
    mod = sb("mod", [P, 2, ADA])
    adab = sb("adab", [P, 2, ADA])
    gain = sb("gain", [P, 4, DC])
    scol = sb("scol", [P, 4, DC])
    g1p = sb("g1p", [P, 4, DC])
    gateb = sb("gateb", [HEADS, 2])
    convw = sb("convw", [P, HEADS, 3])
    mnormc = sb("mnormc", [P, HEADS])
    qkn = sb("qkn", [P, 2])
    keysT = sb("keysT", [P, 2, 2, NKEYS])
    cvec = sb("cvec", [P, D])
    adacol = sb("adacol", [P, 2])
    grant = sb("grant", [P, 1])
    ada_w = sb("ada_w", [P, 2, D])
    raw = sb("raw", [P, RING, D])
    w_hi = sb("w_hi", [P, RING, D], F32R)
    w_lo = sb("w_lo", [P, RING, D], F32R)
    xT = sb("xT", [P, DC, SEQ])
    h_hi = sb("h_hi", [P, DC, SEQ], F32R)
    h_lo = sb("h_lo", [P, DC, SEQ], F32R)
    arena = place[0]

    KB = 1024
    ada_first = sb("ada_first", [P, 2 * DC, D])

    place[0] = arena + 64 * KB
    sq = sb("sq", [P, 2, SEQ])
    acc = sb("acc", [P, SEQ])
    rstd = sb("rstd", [P, SEQ])
    hw = sb("hw", [P, 2, SEQ])

    place[0] = arena
    qT = sb("qT", [P, HEADS, SEQ])
    kT = sb("kT", [P, HEADS, SEQ])
    vT = sb("vT", [P, HEADS, SEQ])
    oT = sb("oT", [P, HEADS, SEQ])
    temp_at = place[0]
    cbT = sb("cbT", [P, HEADS, SEQ])
    ccT = sb("ccT", [P, HEADS, SEQ])
    chT = sb("chT", [P, HEADS, SEQ])
    rrow = sb("rrow", [HEADS, CH, P])
    mrow = sb("mrow", [HEADS, CH, P])
    iwrow = sb("iwrow", [HEADS, CH, P])
    emrow = sb("emrow", [HEADS, CH, P])
    wrow = rrow
    v_nat = sb("v_nat", [P, CH, 2 * P])
    k_nat = sb("k_nat", [P, CH - 1, P])
    state = sb("state", [P, CH - 1, 2 * P])
    gcols = sb("gcols", [P, 2, CH, HEADS])
    decay_b = sb("decay_b", [P, HEADS, CH])
    small = sb("small", [HEADS, 4, CH + 1])
    pt = sb("pt", [P, SEQ])
    qw, den_w = kT, vT
    place[0] = temp_at
    li = sb("li", [HEADS, CH, P])
    lf = sb("lf", [HEADS, CH, P])
    t1 = sb("t1", [HEADS, CH, P])
    scanb = sb("scanb", [HEADS, 2, CH, P + P // 2])
    scanm = sb("scanm", [HEADS, 2, CH, P + P // 2])
    assert place[0] <= temp_at + 3 * HEADS * SEQ * 4

    place[0] = arena
    aq = sb("aq", [P, DC, SEQ])
    ak = sb("ak", [P, DC, SEQ])
    av = sb("av", [P, CH, D])
    work_at = place[0]
    qf = sb("qf", [P, 2, SEQ])
    qsq = sb("qsq", [P, 2, SEQ])
    qrs = sb("qrs", [P, SEQ])
    place[0] = work_at
    sp = sb("sp", [P, 2, CH, SEQ])
    att = sb("att", [P, CH, SEQ])
    sp_hi = sb("sp_hi", [P, CH, SEQ], F32R)
    sp_lo = sb("sp_lo", [P, CH, SEQ], F32R)
    negtri_r = sb("negtri_r", [P, P], F32R)
    negones_r = sb("negones_r", [P, P], F32R)

    place[0] = arena
    sc = sb("sc", [P, N_WQ, CH, NKEYS])
    place[0] = arena
    i16f = sb("i16f", [P, CH, PH, 2, TOPK])
    pos = sb("pos", [P, 2, CH, PH, TOPK], U32)
    posf = sb("posf", [P, 2, CH, PH, TOPK])
    pick = sb("pick", [P, PH, TOPK, TOPK])
    place[0] = arena + N_WQ * SEQ * 4
    qs = sb("qs", [P, 2, SEQ])
    sc2 = sb("sc2", [P, CH, NKEYS])
    v16 = sb("v16", [P, CH, PH, 2, TOPK])
    i16 = sb("i16", [P, CH, PH, 2, TOPK], U32)
    cand = sb("cand", [P, CH, TOPK * TOPK])
    cand2 = sb("cand2", [P, CH, TOPK * TOPK])
    topv = sb("topv", [P, CH, PH, TOPK])
    topi = sb("topi", [P, CH, PH, TOPK], U32)
    ex = sb("ex", [P, 3, CH, PH, TOPK])
    red = sb("red", [P, CH, PH])
    assert place[0] <= limit - 4 * SEQ * 4
    place[0] = arena
    stage = sb("stage", [P, 2, NKEYS, BATCH])
    exT = sb("exT", [P, 5, SEQ])
    one1 = sb("one1", [P, 2, 4, NKEYS], BF16)
    one2 = sb("one2", [P, 2, 4, 3, NKEYS], BF16)
    part = one2[:].rearrange("p a b c d -> p (a b c d)")[:, 0:SEQ]
    place[0] = limit - 4 * SEQ * 4 - (limit % 64)
    assert place[0] >= arena + 64 * 1024 + 5 * SEQ * 4 + 8 * 1024 - 64
    gel = sb("gel", [P, 4, SEQ])

    place[0] = arena
    a_hi = sb("a_hi", [P, 2, GROUP, SEQ], F32R)
    a_lo = sb("a_lo", [P, 2, GROUP, SEQ], F32R)
    gates = sb("gates", [P, 2, NBATCH, UNIT, BATCH])
    gin = sb("gin", [P, 2, UNIT, SEQ])
    assert place[0] <= limit - 4 * SEQ * 4 - (limit % 64)

    g_dram = [nc.dram_tensor(f"g_dram{l}", (NBATCH, P, NKEYS, BATCH), F32, kind="Internal").ap()
              for l in range(2)]
    gel_dram = [nc.dram_tensor(f"gel_dram{l}", (NKEYS, P, SEQ), F32, kind="Internal").ap() for l in range(2)]

    bank = [ctx.enter_context(nc.psum_tensor(f"bank{i}", [P, SEQ], F32)) for i in range(RING)]
    misc = [ctx.enter_context(nc.psum_tensor(f"misc{i}", [P, SEQ], F32)) for i in range(4)]

    sems = {}

    def S(name):
        if name not in sems:
            sems[name] = ctx.enter_context(nc.semaphore(name))
        return sems[name]

    landed = [S(f"landed{i}") for i in range(RING)]
    split_hi, split_lo, tile_done = S("split_hi"), S("split_lo"), S("tile_done")
    emptied_sem = {"a": S("emptied_a"), "d": S("emptied_d")}

    def wait(eng, sem, value):
        if isinstance(value, int) and value <= 0:
            return
        eng.wait_ge(sem, value)

    def zq(h, j, n):
        b = (bank, misc)[h % 2][min(j, 2)]
        return b[:, 0:P] if j == 3 else b[:, n * P:]

    def obank(h):
        return (bank, misc)[h % 2][3]

    together = (1, 2, 4, 4)

    block = ctx.enter_context(nc.Block())

    @block.sync
    def _(sp_):
        def load(i, s):
            sp_.dma_start(raw[:, s, :], stream[ds(i * RING + s, 1), :, :].rearrange("a p n -> p (a n)")
                          ).then_inc(landed[s], 16)

        for s in range(RING):
            load(0, s)
        full = N_TILES // RING
        with sp_.Fori(1, full) as i:
            for s in range(RING):
                sp_.wait_ge(split_lo, i * RING + s - RING + 1)
                load(i, s)
        for t in range(full * RING, N_TILES):
            sp_.wait_ge(split_lo, t - RING + 1)
            load(full, t - full * RING)
        sp_.wait_ge(S("out_stored"), 16 * DC)

    @block.gpsimd
    def _(pool):
        def link(ins, n=[0]):
            n[0] += 1
            ins.then_inc(S("pool_link"), 1)
            pool.wait_ge(S("pool_link"), n[0])

        for t, v in ((ident, 0.0), (identb, 0.0), (ones, 1.0), (halfones, 1.0), (negtri, -1.0),
                     (masked, MASKED), (causal, 1.0), (rowsel, 0.0)):
            last = pool.memset(t[:], v)
        link(last)
        for t in (ident, identb):
            pool.affine_select(out=t[:], in_=t[:], compare_op=ALU.not_equal, fill=1.0, base=0,
                               pattern=[[-1, P]], channel_multiplier=1)
        pool.affine_select(out=rowsel[:], in_=rowsel[:], compare_op=ALU.not_equal, fill=1.0, base=0,
                           pattern=[[-1, HEADS], [0, P]], channel_multiplier=1)
        for t in (negtri, masked):
            pool.affine_select(out=t[:], in_=t[:], compare_op=ALU.is_ge, fill=0.0, base=0,
                               pattern=[[-1, P]], channel_multiplier=1)
        pool.affine_select(out=causal[:], in_=causal[:], compare_op=ALU.is_ge, fill=0.0, base=0,
                           pattern=[[1, P]], channel_multiplier=-1)
        pool.affine_select(out=halfones[:, 0:HD], in_=halfones[:, 0:HD], compare_op=ALU.is_ge, fill=0.0,
                           base=HD - 1, pattern=[[0, HD]], channel_multiplier=-1)
        pool.affine_select(out=halfones[:, HD:], in_=halfones[:, HD:], compare_op=ALU.is_ge, fill=0.0,
                           base=-HD, pattern=[[0, HD]], channel_multiplier=1)
        pool.iota(iota[:], [[1, P]], base=0, channel_multiplier=0,
                  allow_small_or_imprecise_dtypes=True)
        pool.iota(iotab[:], [[1, P]], base=0, channel_multiplier=0,
                  allow_small_or_imprecise_dtypes=True).then_inc(S("const_ready"), 1)

        def low(i, s):
            pool.wait_ge(split_hi, i * RING + s + 1)
            pool.tensor_tensor(w_lo[:, s, :], raw[:, s, :], w_hi[:, s, :].bitcast(F32),
                               ALU.subtract).then_inc(split_lo, 1)

        full = N_TILES // RING
        with pool.Fori(0, full) as i:
            for s in range(RING):
                low(i, s)
        for t in range(full * RING, N_TILES):
            low(full, t - full * RING)

    @block.scalar
    def _(act):
        def high(t, off=0):
            if t >= N_TILES:
                return
            s = t % RING
            act.wait_ge(landed[s], 16 * (t // RING + 1) + off * (16 // RING))
            wait(act, tile_done, t - RING + 1 + off)
            act.activation(w_hi[:, s, :], raw[:, s, :], ACT.Copy).then_inc(split_hi, 1)

        def link(ins, n=[0]):
            n[0] += 1
            ins.then_inc(S("act_link"), 1)
            act.wait_ge(S("act_link"), n[0])

        def square(tag, k, x_ready):
            act.wait_ge(*x_ready)
            wait(act, S(tag + "_acc"), k - 1)
            act.activation(sq[:, k % 2, :], xT[:, k, :], ACT.Square).then_inc(S(tag + "_sq"), 1)

        small_in = [(xT[:], x_t), (cvec[:], c.partition_broadcast(P)), (adab[:], ada_b), (gain[:], gains),
                    (gateb[:], gate_b), (convw[:], conv_w), (mnormc[:], mnorm), (keysT[:], keys),
                    (qkn[:], qk_norm)]
        act.dma_start(small_in[0][0], small_in[0][1]).then_inc(S("x_landed"), 16)
        act.dma_start(small_in[1][0], small_in[1][1]).then_inc(S("c_landed"), 16)
        for n in range(4):
            act.dma_start(ada_first[:, 4 * n:4 * n + 4, :],
                          ada[4 * n:4 * n + 4, :, :].rearrange("a p n -> p a n")
                          ).then_inc(S(f"ada_first{n}"), 16)
        for dst, src in small_in[2:]:
            act.dma_start(dst, src).then_inc(S("small_landed"), 16)

        def ada_load(n, off=0):
            wait(act, S("ada_used"), n - 1 + off)
            src = ada[ds(2 * DC + n + off, 1), :, :].rearrange("a p n -> p (a n)")
            act.dma_start(ada_w[:, n % 2, :], src).then_inc(S(f"ada{n % 2}"), 16)

        act.wait_ge(S("c_landed"), 16)
        act.activation(cvec[:], cvec[:], ACT.Silu).then_inc(S("silu"), 1)
        for k in range(DC):
            square("n0", k, (S("x_landed"), 16))
        for t in range(LEAD):
            high(t)
        ada_load(0)
        ada_load(1)

        def norm(tag):
            act.wait_ge(S(tag + "_var"), 1)
            act.activation(rstd[:], rstd[:], ACT.Sqrt).then_inc(S(tag + "_std"), 1)
            for k in range(DC):
                act.wait_ge(S(tag + "_h"), k + 1)
                act.activation(h_hi[:, k, :], hw[:, k % 2, :], ACT.Copy).then_inc(S(tag + "_hi"), 1)

        norm("n0")

        def row_log():
            act.wait_ge(S("row_abs"), 1)
            act.preload_act_table_set("natural_log_exp_and_others")
            link(act.activation(t1[:], t1[:], ACT.Exp, scale=-1.0))
            act.activation(t1[:], t1[:], ACT.Ln, bias=1.0).then_inc(S("row_ln"), 1)

        def row_exps():
            act.wait_ge(S("row_m"), 1)
            for k in range(CH):
                mp = small[:, 0, k:k + 1]
                act.activation(iwrow[:, k, :], mrow[:, k, :], ACT.Exp, scale=-1.0, bias=mp)
                act.activation(small[:, 3, k:k + 1], small[:, 1, k:k + 1], ACT.Exp, scale=-1.0, bias=mp)
            act.activation(emrow[:], emrow[:], ACT.Exp, scale=-1.0).then_inc(S("row_exp"), 1)
            act.wait_ge(S("r_tp"), 1)
            for k in range(CH):
                last = act.activation(wrow[:, k, :], rrow[:, k, :], ACT.Exp, bias=small[:, 2, k:k + 1])
            last.then_inc(S("row_w"), 1)

        def head_work(h, step):
            if step == 0:
                act.wait_ge(S("v_tp"), h + 1)
                act.activation(v_nat[:, :, 0:P], misc[3][:].rearrange("p (c n) -> p c n", c=CH),
                               ACT.Copy).then_inc(S("v_nat"), 1)
                act.wait_ge(S("d_arg"), h + 1)
                act.activation(pt[:], pt[:], ACT.Exp, scale=-1.0).then_inc(S("d_exp"), 1)
            elif step == 2:
                act.wait_ge(S("den"), h + 1)
                act.activation(den_w[:, h, :], misc[1][:], ACT.Abs).then_inc(S("den_abs"), 1)
                act.wait_ge(S("hm"), h + 1)
                act.activation(qw[:, h, :], qT[:, h, :], ACT.Square).then_inc(S("hm_sq"), 1)
            elif step == 3:
                act.wait_ge(S("hm_var"), h + 1)
                act.activation(den_w[:, h, :], den_w[:, h, :], ACT.Sqrt).then_inc(S("hm_std"), 1)

        for m in range(N_IN):
            t = IN0 + m
            high(t + LEAD)
            if ADA_FROM <= m < ADA_FROM + 15:
                ada_load(2 * (m - ADA_FROM) + 2)
                ada_load(2 * (m - ADA_FROM) + 3)
            act.wait_ge(tile_done, t + 1)
            b = bank[t % RING]
            e = emptied_sem["a"]
            which, k = divmod(m - 1, 4)
            if m == 0:
                act.activation(li[:], b[0:HEADS, :].rearrange("p (c n) -> p c n", c=CH), ACT.Copy)
                act.activation(lf[:], b[32:32 + HEADS, :].rearrange("p (c n) -> p c n", c=CH), ACT.Copy
                               ).then_inc(e, 1)
            elif which == 0:
                act.activation(qT[:, k, :], b[:], ACT.Copy, scale=float(P) ** -0.5).then_inc(e, 1)
            elif which == 6:
                act.activation(oT[:, k, :], b[:], ACT.Sigmoid).then_inc(e, 1)
            else:
                act.activation((kT, vT, cbT, ccT, chT)[which - 1][:, k, :], b[:], ACT.Copy).then_inc(e, 1)
            if m == 1:
                row_log()
            if m == 8:
                row_exps()
            if m >= HEADS_FROM:
                head_work(*divmod(m - HEADS_FROM, 4))
        for k in range(HEADS):
            act.wait_ge(S("conv"), k + 1)
            act.activation(h_hi[:, HEADS + k, :], chT[:, k, :], ACT.Copy).then_inc(S("conv_hi"), 1)
        for h in range(HEADS):
            act.wait_ge(S("mix"), h + 1)
            act.activation(h_hi[:, h, :], qT[:, h, :], ACT.Copy).then_inc(S("mix_hi"), 1)

        def projected_out(layer):
            for m in range(N_OUT):
                t = OUTP[layer] + m
                high(t + LEAD)
                square(f"f{layer}", m, (emptied_sem["d"], emptied("d", t)))

        def peer(layer):
            L = str(layer)
            norm("f" + L)

            def scores_out(m):
                act.wait_ge(S("scores" + L), m + 1)
                act.activation(sc[:, m, :, :], misc[m % 2][:].rearrange("p (c n) -> p c n", c=CH),
                               ACT.Copy).then_inc(S("sc" + L), 1)

            for m in range(N_WQ):
                t = WQ[layer] + m
                high(t + LEAD)
                act.wait_ge(tile_done, t + 1)
                wait(act, S("scores" + L), m - 1)
                act.activation(qs[:, m % 2, :], bank[t % RING][:], ACT.Copy
                               ).then_inc(emptied_sem["a"], 1)
                if m:
                    scores_out(m - 1)
            scores_out(N_WQ - 1)
            t0 = DENSE[layer]
            stored = [S(f"gel_stored{L}{s}") for s in range(4)]

            def u_tile(n, off=0):
                t, s = t0 + n, n % 4
                high(t + LEAD, off)
                act.wait_ge(tile_done, t + 1 + off)
                wait(act, stored[s], 16 * (n // 4) + off * 4)
                act.activation(gel[:, s, :], bank[t % RING][:], ACT.Gelu).then_inc(emptied_sem["a"], 1)
                act.wait_ge(emptied_sem["a"], emptied("a", t) + off)
                act.dma_start(gel_dram[layer][ds(n + off, 1)].rearrange("a p t -> p (a t)"), gel[:, s, :]
                              ).then_inc(stored[s], 16)

            for n in range(4):
                u_tile(n)
            first = 24
            with act.Fori(0, (first - 4) // 4) as i:
                for n in range(4, 8):
                    u_tile(n, i * 4)
            for n in range(first, first + 4):
                u_tile(n)
            act.wait_ge(S("gate_arg" + L), 1)
            act.activation(ex[:, 2, :, :], ex[:, 2, :, :], ACT.Exp).then_inc(S("gate_exp" + L), 1)
            with act.Fori(0, (U_EARLY - first - 4) // 4) as i:
                for n in range(first + 4, first + 8):
                    u_tile(n, i * 4)
            act.wait_ge(S("ex_tp" + L), 3)
            for n in range(3):
                act.activation(exT[:, n, :], misc[n][:], ACT.Copy).then_inc(S("exT" + L), 1)
            link(act.activation(grant[:], ones[:, 0:1], ACT.Copy))
            act.activation(grant[:], ones[:, 0:1], ACT.Copy).then_inc(S("g_out" + L), 4)
            for s in range(2):
                act.wait_ge(S("g_out" + L), 4)
                if s:
                    act.wait_ge(S(f"stored{L}0"), 16)
                act.activation(grant[:], ones[:, 0:1], ACT.Copy).then_inc(S(f"stored{L}{s}"), 16)
            quads = BATCH // 4
            with act.Fori(0, NBATCH // 2) as i:
                for q in range(2 * quads):
                    s = q // quads
                    if q % 2 == 0:
                        u_tile(U_EARLY + q // 2, i * quads)
                    act.wait_ge(S("g_mm" + L), i * (2 * quads) + q + 3)
                    if q % quads == 0:
                        act.wait_ge(S(f"stored{L}{s}"), i * 16 + 16)
                    act.activation(stage[:, s, :, 4 * (q % quads):4 * (q % quads) + 4],
                                   misc[q % 4][:].rearrange("p (t e) -> p e t", t=4),
                                   ACT.Copy).then_inc(S("g_out" + L), 1)
                    if q % quads == quads - 1:
                        act.wait_ge(S("g_out" + L), i * (2 * quads) + q + 5)
                        act.dma_start(g_dram[layer][ds(i * 2 + s, 1)].rearrange("a p e t -> p (a e t)"),
                                      stage[:, s, :, :].rearrange("p e t -> p (e t)")
                                      ).then_inc(S(f"stored{L}{s}"), 16)

            def load_unit(u, off=0):
                if not isinstance(off, int) or u >= 2:
                    act.wait_ge(S("acted" + L), UNIT * (u - 1) + off * UNIT)
                b = u % 2
                act.dma_start(gates[:, b, :, :, :], g_dram[layer].rearrange("b p e t -> p b e t")[
                    :, :, ds(u * UNIT + off * UNIT, UNIT), :]).then_inc(S(f"unit{L}{b}"), 16)
                act.dma_start(gin[:, b, :, :], gel_dram[layer].rearrange("e p t -> p e t")[
                    :, ds(u * UNIT + off * UNIT, UNIT), :]).then_inc(S(f"unit{L}{b}"), 16)

            tail = U_EARLY + U_GATES
            for n in range(tail, NKEYS):
                u_tile(n)
                if n == tail + 7:
                    for s in range(2):
                        act.wait_ge(S(f"stored{L}{s}"), 16 * (NBATCH // 2) + 16)
                    for s in range(4):
                        act.wait_ge(stored[s], 16 * (2 * GROUP // 4))
                if n >= tail + 7 and n % 2 and (n - tail - 7) // 2 <= GROUP // UNIT:
                    load_unit((n - tail - 7) // 2)
            for s in range(4):
                act.wait_ge(stored[s], 16 * (NKEYS // 4))

            def v_tiles(g, first_ada, i=0, turn=0):
                for k in range(GROUP):
                    high(t0 + NKEYS + g * GROUP + k + LEAD, i * 16 if turn else 0)
                    u = ((g + 1) * GROUP + k) // UNIT + 1
                    if k % UNIT == 0 and (turn or u < NKEYS // UNIT):
                        load_unit(u, i * (2 * GROUP // UNIT) if turn else 0)
                    if layer == 0 and k in (0, 2, 4):
                        ada_load(first_ada + k // 2, i * 6 if turn else 0)
                    if layer == 0 and not turn and g == NGROUP - 1:
                        square("n1", k, (emptied_sem["d"], emptied("d", t0 + NKEYS + g * GROUP + k)))

            v_tiles(0, 4 * DC)
            with act.Fori(0, V_TURNS) as i:
                for half in range(2):
                    v_tiles(1 + half, 4 * DC + 3 + 3 * half, i, 1)
            for g in range(1 + 2 * V_TURNS, NGROUP):
                v_tiles(g, 4 * DC + 3 * g)

        projected_out(0)
        peer(0)

        norm("n1")

        def root(m):
            act.wait_ge(S("qk_var"), m + 1)
            act.activation(qrs[:], qrs[:], ACT.Sqrt).then_inc(S("qk_std"), 1)

        def v_out(k):
            act.wait_ge(S("av_tp"), k + 1)
            act.activation(av[:, :, k * P:(k + 1) * P], misc[k % 2][:].rearrange("p (c n) -> p c n", c=CH),
                           ACT.Copy).then_inc(S("av_out"), 1)

        for m in range(N_QKV):
            t = QKV1 + m
            high(t + LEAD)
            act.wait_ge(tile_done, t + 1)
            if m < 2 * DC:
                wait(act, S("qk_done"), m - 1)
                act.activation(qsq[:, m % 2, :], bank[t % RING][:], ACT.Square)
                act.activation(qf[:, m % 2, :], bank[t % RING][:], ACT.Copy
                               ).then_inc(emptied_sem["a"], 1)
            else:
                if m < 2 * DC + 2:
                    act.wait_ge(S("qk_done"), m - 1)
                wait(act, S("av_tp"), m - 2 * DC - 1)
                act.activation(qf[:, m % 2, :], bank[t % RING][:], ACT.Copy
                               ).then_inc(emptied_sem["a"], 1)
            if 1 <= m <= 2 * DC:
                root(m - 1)
            if m > 2 * DC:
                v_out(m - 2 * DC - 1)
        v_out(DC - 1)

        act.preload_act_table_set("natural_log_exp_and_others")
        act.activation(negtri_r[:], negtri[:], ACT.Copy)
        act.activation(negones_r[:], ones[:], ACT.Copy, scale=-1.0).then_inc(S("neg"), 1)

        def sticks(h):
            for j in range(CH):
                act.wait_ge(S("z_abs"), CH * h + j + 1)
                zs = sp[:, h % 2, j, j * P:]
                act.activation(zs, zs, ACT.Exp, scale=-1.0).then_inc(S("z_exp"), 1)
                act.wait_ge(S("z_exp"), CH * h + j + 1)
                act.activation(zs, zs, ACT.Ln, bias=1.0).then_inc(S("z_ln"), 1)

        def stick_highs(h):
            wait(act, S("logw"), CH * h)
            for j in range(CH):
                act.wait_ge(S("sp"), CH * h + j + 1)
                act.activation(sp_hi[:, j, j * P:], sp[:, h % 2, j, j * P:], ACT.Copy
                               ).then_inc(S("sp_hi"), 1)

        def weights(h):
            for j in range(CH):
                act.wait_ge(S("logw"), CH * h + together[j])
                wait(act, S("att_out"), h)
                act.activation(att[:, j, j * P:], zq(h, j, j), ACT.Exp).then_inc(S("att"), 1)

        def mixed(h):
            o = HD * (h % 2)
            act.wait_ge(S("att_out"), h + 1)
            act.activation(h_hi[o:o + HD, h // 2, :], obank(h)[o:o + HD, :], ACT.Copy
                           ).then_inc(S("o_hi"), 1)

        sticks(0)
        stick_highs(0)
        for h in range(SB_HEADS):
            if h + 1 < SB_HEADS:
                sticks(h + 1)
            if h:
                mixed(h - 1)
            weights(h)
            if h + 1 < SB_HEADS:
                stick_highs(h + 1)
        mixed(SB_HEADS - 1)
        projected_out(1)
        peer(1)
        for m in range(DC):
            act.wait_ge(emptied_sem["d"], emptied("d", N_TILES - 1) - DC + m + 1)
            act.dma_start(out_t[:, m, :], xT[:, m, :]).then_inc(S("out_stored"), 16)

    @block.tensor
    def _(pe):
        def tile(t, hi, lo, off=0, ready=None):
            b = bank[t % RING]
            pe.wait_ge(split_lo, t + 1 + off)
            if t >= RING:
                k = EVAC[t - RING]
                pe.wait_ge(emptied_sem[k], emptied(k, t - RING) + off)
            for k in range(DC):
                if ready:
                    ready(k)
                wh = w_hi[:, t % RING, k * P:(k + 1) * P]
                wl = w_lo[:, t % RING, k * P:(k + 1) * P]
                pe.matmul(b[:], wh, hi(k), start=(k == 0), stop=False)
                pe.matmul(b[:], wh, lo(k), start=False, stop=False)
                mm = pe.matmul(b[:], wl, hi(k), start=False, stop=(k == DC - 1))
            mm.then_inc(tile_done, 1)

        def h_tile(t, **kw):
            tile(t, lambda k: h_hi[:, k, :], lambda k: h_lo[:, k, :], **kw)

        def norm(tag):
            pe.wait_ge(S(tag + "_acc"), DC)
            pe.matmul(misc[0][:], ones[:], acc[:], start=True, stop=True).then_inc(S(tag + "_sum"), 1)

        pe.wait_ge(S("const_ready"), 1)
        norm("n0")
        def head_work(h, step):
            if step == 0:
                wait(pe, S("hm_var"), h)
                for k in range(CH - 1):
                    last = pe.transpose(misc[2][:, k * P:(k + 1) * P], kT[:, h, k * P:(k + 1) * P], ident[:])
                last.then_inc(S("k_tp"), 1)
                for k in range(CH):
                    last = pe.transpose(misc[3][:, k * P:(k + 1) * P], vT[:, h, k * P:(k + 1) * P], ident[:])
                last.then_inc(S("v_tp"), 1)
                pe.matmul(misc[0][:], rowsel[:, h, :], mrow[:], start=True, stop=True).then_inc(S("m_mm"), 1)
                for k in range(CH):
                    c_ = slice(k * P, (k + 1) * P)
                    last = pe.matmul(misc[1][:, c_], kT[:, h, c_], qT[:, h, c_], start=True, stop=True)
                last.then_inc(S("qk_mm"), 1)
            elif step == 1:
                pe.wait_ge(S("kw"), h + 1)
                pe.matmul(misc[2][:], rowsel[:, h, :], iwrow[:], start=True, stop=True
                          ).then_inc(S("iw_mm"), 1)
                pe.wait_ge(S("v_nat"), h + 1)
                pe.wait_ge(S("d_arg"), h + 1)
                for k in range(CH - 1):
                    b = (misc[3], misc[3], misc[0])[k]
                    o = (0, 2 * P, 0)[k]
                    last = pe.matmul(b[:, o:o + 2 * P], k_nat[:, k, :], v_nat[:, k, :], start=True, stop=True)
                last.then_inc(S("state_mm"), 1)
            elif step == 2:
                pe.wait_ge(S("pt"), h + 1)
                pe.wait_ge(S("qw"), h + 1)
                pe.wait_ge(S("state"), h + 1)
                for b, vn, st, done in ((misc[1], lambda k: ones[:], P, "den"),
                                        (misc[2], lambda k: v_nat[:, k, 0:P], 0, "num")):
                    for k in range(CH):
                        c_ = slice(k * P, (k + 1) * P)
                        last = pe.matmul(b[:, c_], vn(k), pt[:, c_], start=True, stop=(k == 0))
                        if k:
                            last = pe.matmul(b[:, c_], state[:, k - 1, st:st + P], qw[:, h, c_],
                                             start=False, stop=True)
                    last.then_inc(S(done), 1)
                pe.matmul(misc[0][:], rowsel[:, h, :], emrow[:], start=True, stop=True
                          ).then_inc(S("em_mm"), 1)
            else:
                pe.wait_ge(S("hm_sq"), h + 1)
                pe.matmul(misc[3][:], ones[:], qw[:, h, :], start=True, stop=True).then_inc(S("hm_ss"), 1)

        for m in range(N_IN):
            h_tile(IN0 + m, ready=(lambda k: pe.wait_ge(S("n0_lo"), k + 1)) if m == 0 else None)
            if m == 5:
                pe.wait_ge(S("row_r"), 1)
                for k in range(CH):
                    last = pe.transpose(misc[0][:, k * HEADS:(k + 1) * HEADS], rrow[:, k, :],
                                        ident[0:HEADS, 0:HEADS])
                last.then_inc(S("r_tp"), 1)
            if m == 10:
                pe.wait_ge(S("row_exp"), 1)
                for h in range(HEADS):
                    last = pe.matmul(misc[2][:, h * CH:(h + 1) * CH], rowsel[:, h, :], small[:, 3, 0:CH],
                                     start=True, stop=True)
                last.then_inc(S("decay_mm"), 1)
                pe.wait_ge(S("row_w"), 1)
                for k in range(CH):
                    last = pe.transpose(misc[1][:, k * HEADS:(k + 1) * HEADS], wrow[:, k, :],
                                        ident[0:HEADS, 0:HEADS])
                last.then_inc(S("w_tp"), 1)
            if m == HEADS_FROM:
                pe.wait_ge(S("cols"), 3)
                pe.wait_ge(emptied_sem["a"], emptied("a", IN0 + 12))
            if m >= HEADS_FROM:
                head_work(*divmod(m - HEADS_FROM, 4))

        def mixed_ready(k):
            if k < HEADS:
                pe.wait_ge(S("mix_lo"), k + 1)
            else:
                pe.wait_ge(S("conv_lo"), k - HEADS + 1)

        for m in range(N_OUT):
            h_tile(OUT0 + m, ready=mixed_ready if m == 0 else None)

        def peer(layer):
            L = str(layer)
            norm("f" + L)

            def scores(m):
                pe.wait_ge(emptied_sem["a"], emptied("a", WQ[layer] + m))
                wait(pe, S("sc" + L), m - 1)
                for k in range(CH):
                    last = pe.matmul(misc[m % 2][:, k * P:(k + 1) * P], qs[:, m % 2, k * P:(k + 1) * P],
                                     keysT[:, layer, m % 2, :], start=True, stop=True)
                last.then_inc(S("scores" + L), 1)

            for m in range(N_WQ):
                h_tile(WQ[layer] + m, ready=(lambda k: pe.wait_ge(S(f"f{L}_lo"), k + 1)) if m == 0 else None)
                if m:
                    scores(m - 1)
            scores(N_WQ - 1)
            t0 = DENSE[layer]
            for n in range(4):
                h_tile(t0 + n)
            with pe.Fori(0, (U_EARLY - 4) // 4) as i:
                for n in range(4, 8):
                    h_tile(t0 + n, off=i * 4)
            for n in range(3):
                pe.wait_ge(S("ex" + L), n + 1)
                for k in range(CH):
                    last = pe.transpose(misc[n][:, k * P:(k + 1) * P],
                                        ex[:, n, k, :, :].rearrange("p h k -> p (h k)"), ident[:])
                last.then_inc(S("ex_tp" + L), 1)
            with pe.Fori(0, U_GATES // 4) as i:
                for q in range(8):
                    if q % 2 == 0:
                        h_tile(t0 + U_EARLY + q // 2, off=i * 4)
                    pe.wait_ge(S("one" + L), i * 8 + q + 1)
                    pe.wait_ge(S("g_out" + L), i * 8 + q + 1)
                    for u in range(4):
                        for n in range(3):
                            last = pe.matmul(misc[q % 4][:, u * P:(u + 1) * P], one1[:, q % 2, u, :],
                                             one2[:, q % 2, u, n, :], start=(n == 0), stop=(n == 2))
                    last.then_inc(S("g_mm" + L), 1)
            for n in range(U_EARLY + U_GATES, NKEYS):
                h_tile(t0 + n)

            def v_tiles(g, i=0, turn=0):
                pe.wait_ge(S("acted" + L), GROUP * (g + 1) + (i * 16 if turn else 0))
                for k in range(GROUP):
                    tile(t0 + NKEYS + g * GROUP + k, lambda b: a_hi[:, g % 2, b, :],
                         lambda b: a_lo[:, g % 2, b, :], off=i * 16 if turn else 0)

            v_tiles(0)
            with pe.Fori(0, V_TURNS) as i:
                for half in range(2):
                    v_tiles(1 + half, i, 1)
            for g in range(1 + 2 * V_TURNS, NGROUP):
                v_tiles(g)

        peer(0)

        norm("n1")

        def square_sums(m):
            pe.wait_ge(emptied_sem["a"], emptied("a", QKV1 + m))
            wait(pe, S("qk_var"), m - 1)
            pe.matmul(misc[2 + m % 2][:], halfones[:], qsq[:, m % 2, :], start=True, stop=True
                      ).then_inc(S("qk_ss"), 1)

        def turn_v(k):
            pe.wait_ge(emptied_sem["a"], emptied("a", QKV1 + 2 * DC + k))
            wait(pe, S("av_out"), k - 1)
            for j in range(CH):
                last = pe.transpose(misc[k % 2][:, j * P:(j + 1) * P], qf[:, k % 2, j * P:(j + 1) * P],
                                    ident[:])
            last.then_inc(S("av_tp"), 1)

        for m in range(N_QKV):
            h_tile(QKV1 + m, ready=(lambda k: pe.wait_ge(S("n1_lo"), k + 1)) if m == 0 else None)
            if 1 <= m <= 2 * DC:
                square_sums(m - 1)
            if m > 2 * DC:
                turn_v(m - 2 * DC - 1)
        turn_v(DC - 1)
        pe.wait_ge(S("neg"), 1)
        pe.wait_ge(S("qk_done"), 2 * DC)
        pe.wait_ge(S("av_out"), DC)

        def logits(h):
            o, m = HD * (h % 2), h // 2
            for j in range(CH):
                if 2 <= h and j < 3:
                    pe.wait_ge(S("att"), CH * (h - 2) + together[j])
                pe.matmul(zq(h, j, j), ak[o:o + HD, m, j * P:(j + 1) * P], aq[o:o + HD, m, j * P:],
                          start=(j < 3), stop=False, skip_group_check=True)
                last = pe.matmul(zq(h, j, j)[:, 0:P], identb[:], masked[:], start=False, stop=True,
                                 skip_group_check=True)
                if j != 2:
                    last.then_inc(S("z"), 2 if j == 3 else 1)

        def log_weights(h):
            pe.wait_ge(S("sp_hi"), CH * (h + 1))
            pe.wait_ge(S("sp_lo"), CH * (h + 1))
            for j in range(CH):
                for part_ in (sp_hi, sp_lo):
                    last = pe.matmul(zq(h, j, j), negtri_r[:], part_[:, j, j * P:], start=False, stop=True,
                                     skip_group_check=True)
                    for n in range(j + 1, CH):
                        last = pe.matmul(zq(h, j, n), negones_r[:], part_[:, n, n * P:], start=False,
                                         stop=True, skip_group_check=True)
                if j != 2:
                    last.then_inc(S("logw"), 2 if j == 3 else 1)

        def weighted(h):
            o = HD * (h % 2)
            if h >= 2:
                pe.wait_ge(S("o_hi"), h - 1)
                pe.wait_ge(S("o_lo"), h - 1)
            for j in range(CH):
                pe.wait_ge(S("att"), CH * h + j + 1)
                last = pe.matmul(obank(h)[o:o + HD, j * P:], av[:, j, h * HD:(h + 1) * HD],
                                 att[:, j, j * P:], start=(j == 0), stop=(j == CH - 1), skip_group_check=True)
            last.then_inc(S("att_out"), 1)

        logits(0)
        for h in range(SB_HEADS):
            if h + 1 < SB_HEADS:
                logits(h + 1)
            if h:
                weighted(h - 1)
            log_weights(h)
        weighted(SB_HEADS - 1)
        pe.wait_ge(S("o_lo"), SB_HEADS)
        for m in range(N_OUT):
            h_tile(OUT1 + m)
        peer(1)

    @block.vector
    def _(dve):
        links = [0]

        def link(ins):
            links[0] += 1
            ins.then_inc(S("dve_link"), 1)
            dve.wait_ge(S("dve_link"), links[0])

        def ada_dot(n, dst, off=0):
            s = n % 2
            dve.wait_ge(S(f"ada{s}"), 16 * (n // 2 + 1) + (off * 8))
            dve.tensor_tensor_reduce(ada_w[:, s, :], ada_w[:, s, :], cvec[:], 1.0, 0.0, ALU.mult, ALU.add,
                                     dst).then_inc(S("ada_used"), 1)

        def columns(n, l, part):
            dve.scalar_tensor_tensor(out=scol[:, n, :], in0=mod[:, l, part + DC:part + 2 * DC], scalar=1.0,
                                     in1=gain[:, n, :], op0=ALU.add, op1=ALU.mult)

        def add_square(tag, k):
            dve.wait_ge(S(tag + "_sq"), k + 1)
            if k == 0:
                dve.tensor_copy(acc[:], sq[:, 0, :]).then_inc(S(tag + "_acc"), 1)
            else:
                dve.wait_ge(S(tag + "_acc"), k)
                dve.tensor_tensor(acc[:], acc[:], sq[:, k % 2, :], ALU.add).then_inc(S(tag + "_acc"), 1)

        def root(tag):
            dve.wait_ge(S(tag + "_sum"), 1)
            dve.tensor_scalar(rstd[:], misc[0][:], 1.0 / D, EPS, ALU.mult, ALU.add).then_inc(S(tag + "_var"), 1)
            dve.wait_ge(S(tag + "_std"), 1)
            link(dve.reciprocal(rstd[:], rstd[:]))

        def norm(tag, n, l, part):
            def low(k):
                dve.wait_ge(S(tag + "_hi"), k + 1)
                dve.tensor_tensor(h_lo[:, k, :], hw[:, k % 2, :], h_hi[:, k, :].bitcast(F32),
                                  ALU.subtract).then_inc(S(tag + "_lo"), 1)

            for k in range(DC + 1):
                if k < DC:
                    wait(dve, S(tag + "_lo"), k - 1)
                    link(dve.tensor_tensor(hw[:, k % 2, :], xT[:, k, :], rstd[:], ALU.mult))
                    dve.tensor_scalar(hw[:, k % 2, :], hw[:, k % 2, :], scol[:, n, k:k + 1],
                                      mod[:, l, part + k:part + k + 1], ALU.mult, ALU.add
                                      ).then_inc(S(tag + "_h"), 1)
                if k:
                    low(k - 1)

        def x_update(t, m, n, off=0):
            dve.wait_ge(tile_done, t + 1 + off)
            if emptied("d", t) > DC:
                dve.wait_ge(emptied_sem["d"], emptied("d", t) - DC + off)
            dve.scalar_tensor_tensor(out=xT[:, m, :], in0=bank[t % RING][:], scalar=g1p[:, n, m:m + 1],
                                     in1=xT[:, m, :], op0=ALU.mult, op1=ALU.add
                                     ).then_inc(emptied_sem["d"], 1)

        dve.wait_ge(S("silu"), 1)
        for k in range(DC):
            add_square("n0", k)
        for n in range(2 * DC):
            if n % 4 == 0:
                dve.wait_ge(S(f"ada_first{n // 4}"), 16)
            last = dve.tensor_tensor_reduce(ada_first[:, n, :], ada_first[:, n, :], cvec[:], 1.0, 0.0,
                                            ALU.mult, ALU.add, mod[:, 0, n:n + 1])
        link(last)
        dve.wait_ge(S("small_landed"), 16 * 7)
        link(dve.tensor_tensor(mod[:, 0, 0:2 * DC], mod[:, 0, 0:2 * DC], adab[:, 0, 0:2 * DC], ALU.add))
        columns(0, 0, 0)
        dve.wait_ge(S("x_landed"), 16)
        link(dve.tensor_scalar(qkn[:, 0:1], qkn[:, 0:1], float(HD) ** -0.5, None, ALU.mult))
        root("n0")
        norm("n0", 0, 0, 0)
        dve.wait_ge(emptied_sem["a"], 1)
        dve.tensor_scalar(li[:], li[:], gateb[:, 0:1], None, ALU.add)
        link(dve.tensor_scalar(lf[:], lf[:], gateb[:, 1:2], None, ALU.add))
        dve.tensor_scalar(t1[:].bitcast(U32), lf[:].bitcast(U32), NO_SIGN, None, ALU.bitwise_and
                          ).then_inc(S("row_abs"), 1)
        H = P // 2
        dve.memset(v_nat[:, :, P:], 1.0)
        dve.memset(scanb[:, :, :, 0:H], 0.0)
        dve.memset(scanm[:, :, :, 0:H], LOWEST)
        link(dve.memset(small[:], 0.0))
        dve.wait_ge(S("row_ln"), 1)
        link(dve.scalar_tensor_tensor(out=scanb[:, 0, :, H:], in0=lf[:], scalar=0.0, in1=t1[:],
                                      op0=ALU.min, op1=ALU.subtract))

        def scan(buf, op):
            for n in range(7):
                a, b, w = n % 2, (n + 1) % 2, 1 << n
                link(dve.tensor_tensor(buf[:, b, :, H:], buf[:, a, :, H:], buf[:, a, :, H - w:H + P - w], op))

        scan(scanb, ALU.add)
        bsum = scanb[:, 1, :, H:]
        link(dve.tensor_tensor(rrow[:], li[:], bsum, ALU.subtract))
        dve.tensor_copy(scanm[:, 0, :, H:], rrow[:]).then_inc(S("row_r"), 1)
        dve.wait_ge(S("row_r"), 1)
        scan(scanm, ALU.max)
        cm = scanm[:, 1, :, H:]
        for k in range(CH):
            link(dve.tensor_tensor(small[:, 1, k:k + 1], small[:, 0, k:k + 1], cm[:, k, P - 1:P], ALU.max))
            link(dve.tensor_tensor(small[:, 0, k + 1:k + 2], small[:, 1, k:k + 1], bsum[:, k, P - 1:P], ALU.add))
        for k in range(CH):
            last = dve.tensor_scalar(mrow[:, k, :], cm[:, k, :], small[:, 0, k:k + 1], None, ALU.max)
        link(last)
        dve.tensor_scalar(small[:, 2, 0:CH], small[:, 1, 0:CH], -1.0, None, ALU.mult)
        dve.tensor_tensor(emrow[:], mrow[:], bsum, ALU.add).then_inc(S("row_m"), 1)
        dve.wait_ge(S("r_tp"), 1)
        dve.tensor_copy(gcols[:, 0, :, :], misc[0][:, 0:CH * HEADS].rearrange("p (c h) -> p c h", c=CH)
                        ).then_inc(S("cols"), 1)
        dve.wait_ge(S("decay_mm"), 1)
        dve.tensor_copy(decay_b[:], misc[2][:, 0:CH * HEADS].rearrange("p (h c) -> p h c", c=CH)
                        ).then_inc(S("cols"), 1)
        dve.wait_ge(S("w_tp"), 1)
        dve.tensor_copy(gcols[:, 1, :, :], misc[1][:, 0:CH * HEADS].rearrange("p (c h) -> p c h", c=CH)
                        ).then_inc(S("cols"), 1)
        dve.wait_ge(S("cols"), 3)

        def by_chunk(ap):
            return ap.rearrange("p (c n) -> p c n", c=CH)

        def head_work(h, step):
            w0, w1, w2, hm = pt[:], qw[:, h, :], den_w[:, h, :], qT[:, h, :]
            if step == 0:
                dve.wait_ge(S("k_tp"), h + 1)
                for k in range(CH - 1):
                    last = dve.tensor_scalar(k_nat[:, k, :], misc[2][:, k * P:(k + 1) * P],
                                             gcols[:, 1, k, h:h + 1], None, ALU.mult)
                last.then_inc(S("kw"), 1)
                dve.wait_ge(S("m_mm"), h + 1)
                link(dve.tensor_tensor(by_chunk(w0), by_chunk(misc[0][:]),
                                       gcols[:, 0, :, h:h + 1].to_broadcast([P, CH, P]), ALU.subtract))
                dve.tensor_scalar(w0, w0, 0.0, None, ALU.max).then_inc(S("d_arg"), 1)
                dve.wait_ge(S("d_exp"), h + 1)
                dve.wait_ge(S("qk_mm"), h + 1)
                link(dve.tensor_tensor(w0, w0, misc[1][:], ALU.mult))
                dve.tensor_tensor(by_chunk(w0), by_chunk(w0), causal[:].unsqueeze(1).to_broadcast([P, CH, P]),
                                  ALU.mult).then_inc(S("pt"), 1)
            elif step == 1:
                dve.wait_ge(S("iw_mm"), h + 1)
                dve.tensor_tensor(w1, qT[:, h, :], misc[2][:], ALU.mult).then_inc(S("qw"), 1)
                dve.wait_ge(S("state_mm"), h + 1)
                link(dve.tensor_copy(state[:, 0, :], misc[3][:, 0:2 * P]))
                for k in range(1, CH - 1):
                    src = misc[3][:, 2 * P:] if k == 1 else misc[0][:, 0:2 * P]
                    last = dve.scalar_tensor_tensor(out=state[:, k, :], in0=state[:, k - 1, :],
                                                    scalar=decay_b[:, h, k:k + 1], in1=src, op0=ALU.mult,
                                                    op1=ALU.add)
                    if k < CH - 2:
                        link(last)
                last.then_inc(S("state"), 1)
            elif step == 2:
                dve.wait_ge(S("den_abs"), h + 1)
                dve.wait_ge(S("em_mm"), h + 1)
                link(dve.tensor_tensor(w2, w2, misc[0][:], ALU.max))
                link(dve.reciprocal(w2, w2))
                dve.wait_ge(S("num"), h + 1)
                dve.tensor_tensor(hm, misc[2][:], w2, ALU.mult).then_inc(S("hm"), 1)
            else:
                dve.wait_ge(S("hm"), h + 1)
                dve.wait_ge(S("hm_ss"), h + 1)
                dve.tensor_scalar(w2, misc[3][:], 1.0 / P, EPS, ALU.mult, ALU.add).then_inc(S("hm_var"), 1)
                dve.wait_ge(S("hm_std"), h + 1)
                link(dve.reciprocal(w2, w2))
                link(dve.tensor_tensor(hm, hm, w2, ALU.mult))

        def convolve(k):
            dve.wait_ge(emptied_sem["a"], 22 + k)
            u, y = ccT[:, k, :], chT[:, k, :]
            link(dve.tensor_tensor(u, ccT[:, k, :], chT[:, k, :], ALU.mult))
            link(dve.tensor_scalar(y, u, convw[:, k, 2:3], None, ALU.mult))
            for n in (1, 2):
                link(dve.scalar_tensor_tensor(out=chT[:, k, n:], in0=ccT[:, k, 0:SEQ - n],
                                              scalar=convw[:, k, 2 - n:3 - n], in1=chT[:, k, n:],
                                              op0=ALU.mult, op1=ALU.add))
            dve.tensor_tensor(y, y, cbT[:, k, :], ALU.mult).then_inc(S("conv"), 1)

        for m in range(ADA_FROM, N_IN):
            if m < ADA_FROM + 16:
                for n in (2 * (m - ADA_FROM), 2 * (m - ADA_FROM) + 1):
                    ada_dot(n, mod[:, 0, 2 * DC + n:2 * DC + n + 1])
            if m >= HEADS_FROM:
                head_work(*divmod(m - HEADS_FROM, 4))
            if m >= N_IN - HEADS:
                convolve(m - N_IN + HEADS)
        dve.wait_ge(S("ada_used"), 4 * DC)
        link(dve.tensor_tensor(mod[:, 0, 2 * DC:], mod[:, 0, 2 * DC:], adab[:, 0, 2 * DC:], ALU.add))
        dve.tensor_scalar(g1p[:, 0, :], mod[:, 0, 2 * DC:3 * DC], 1.0, None, ALU.add)
        dve.tensor_scalar(g1p[:, 1, :], mod[:, 0, 5 * DC:6 * DC], 1.0, None, ALU.add)
        columns(1, 0, 3 * DC)
        dve.wait_ge(emptied_sem["a"], N_IN)
        for h in range(HEADS):
            dve.scalar_tensor_tensor(out=qT[:, h, :], in0=qT[:, h, :], scalar=mnormc[:, h:h + 1],
                                     in1=oT[:, h, :], op0=ALU.mult, op1=ALU.mult).then_inc(S("mix"), 1)
        for k in range(HEADS):
            dve.wait_ge(S("conv_hi"), k + 1)
            dve.tensor_tensor(h_lo[:, HEADS + k, :], chT[:, k, :], h_hi[:, HEADS + k, :].bitcast(F32),
                              ALU.subtract).then_inc(S("conv_lo"), 1)
        for h in range(HEADS):
            dve.wait_ge(S("mix"), h + 1)
            dve.wait_ge(S("mix_hi"), h + 1)
            dve.tensor_tensor(h_lo[:, h, :], qT[:, h, :], h_hi[:, h, :].bitcast(F32), ALU.subtract
                              ).then_inc(S("mix_lo"), 1)

        def output(layer):
            for m in range(N_OUT):
                x_update(OUTP[layer] + m, m, 2 * layer)
                if m:
                    add_square(f"f{layer}", m - 1)
            add_square(f"f{layer}", N_OUT - 1)
            root(f"f{layer}")

        def peer(layer):
            L = str(layer)
            norm("f" + L, 2 * layer + 1, layer, 3 * DC)

            def step(instructions):
                for ins in instructions:
                    last = ins()
                link(last)

            def top16(values, spare, v, i):
                r = range(CH)
                step([lambda c=c: dve.max(v(c)[:, 0:8], values(c)) for c in r])
                step([lambda c=c: dve.max_index(i(c)[:, 0:8], v(c)[:, 0:8], values(c)) for c in r] +
                     [lambda c=c: dve.match_replace(spare(c), v(c)[:, 0:8], values(c), LOWEST) for c in r])
                step([lambda c=c: dve.max(v(c)[:, 8:16], spare(c)) for c in r])
                return [lambda c=c: dve.max_index(i(c)[:, 8:16], v(c)[:, 8:16], spare(c)) for c in r]

            def rank(m):
                h, half = m // 2, m % 2
                dve.wait_ge(S("sc" + L), m + 1)
                for ins in top16(lambda c: sc[:, m, c, :], lambda c: sc2[:, c, :],
                                 lambda c: v16[:, c, h, half, :], lambda c: i16[:, c, h, half, :]):
                    last = ins()
                last.then_inc(S("ranked" + L), 1)
                dve.wait_ge(S("ranked" + L), m + 1)

            def choose(h):
                link(dve.tensor_tensor(
                    cand[:].rearrange("p c (a b) -> p c a b", a=TOPK),
                    v16[:, :, h, 0, :].unsqueeze(3).to_broadcast([P, CH, TOPK, TOPK]),
                    v16[:, :, h, 1, :].unsqueeze(2).to_broadcast([P, CH, TOPK, TOPK]), ALU.add))
                step(top16(lambda c: cand[:, c, :], lambda c: cand2[:, c, :],
                           lambda c: topv[:, c, h, :], lambda c: topi[:, c, h, :]))

            for m in range(N_WQ):
                rank(m)
                if m % 2:
                    choose(m // 2)
            dve.tensor_tensor(ex[:, 2, :, :, :], topv[:], topv[:, :, :, 0:1].to_broadcast([P, CH, PH, TOPK]),
                              ALU.subtract).then_inc(S("gate_arg" + L), 1)
            dve.tensor_scalar(pos[:, 0], topi[:], 4, None, ALU.logical_shift_right)
            link(dve.tensor_scalar(pos[:, 1], topi[:], TOPK - 1, None, ALU.bitwise_and))
            dve.tensor_copy(posf[:], pos[:])
            link(dve.tensor_copy(i16f[:], i16[:]))
            for half in range(2):
                for c_ in range(CH):
                    where = posf[:, half, c_, :, :].unsqueeze(3).to_broadcast([P, PH, TOPK, TOPK])
                    index = i16f[:, c_, :, half, :].unsqueeze(2).to_broadcast([P, PH, TOPK, TOPK])
                    sixteen = iota[:, 0:TOPK].unsqueeze(1).unsqueeze(1).to_broadcast([P, PH, TOPK, TOPK])
                    link(dve.tensor_tensor(pick[:], where, sixteen, ALU.is_equal))
                    link(dve.tensor_tensor(pick[:], pick[:], index, ALU.mult))
                    last = dve.tensor_reduce(ex[:, half, c_, :, :], pick[:], AX_X, ALU.add)
                    if c_ < CH - 1:
                        link(last)
                last.then_inc(S("ex" + L), 1)
                dve.wait_ge(S("ex" + L), half + 1)
            dve.wait_ge(S("gate_exp" + L), 1)
            link(dve.tensor_reduce(red[:], ex[:, 2, :, :, :], AX_X, ALU.add))
            link(dve.reciprocal(red[:], red[:]))
            dve.tensor_tensor(ex[:, 2, :, :, :], ex[:, 2, :, :, :],
                              red[:].unsqueeze(3).to_broadcast([P, CH, PH, TOPK]), ALU.mult
                              ).then_inc(S("ex" + L), 1)
            dve.wait_ge(S("exT" + L), 3)
            for n in (2, 3):
                link(dve.tensor_copy(part, exT[:, n, :]))
                link(dve.tensor_tensor(exT[:, n + 1, :], exT[:, n, :], part, ALU.subtract))
                link(dve.tensor_copy(exT[:, n, :], part))
            dve.memset(one1[:, 0, 0, 0:8], 0.0).then_inc(S("g_mm" + L), 2)
            with dve.Fori(0, SEQ // 16) as i:
                for q in range(4):
                    dve.wait_ge(S("g_mm" + L), i * 4 + q + 1)
                    dve.tensor_tensor(one1[:, q % 2, :, :], iotab[:].unsqueeze(1).to_broadcast([P, 4, NKEYS]),
                                      exT[:, 0, ds(i * 16 + 4 * q, 4)].unsqueeze(2).to_broadcast([P, 4, NKEYS]),
                                      ALU.is_equal)
                    for u in range(4):
                        tok = ds(i * 16 + 4 * q + u, 1)
                        for n in range(3):
                            last = dve.tensor_scalar(one2[:, q % 2, u, n, :], iotab[:], exT[:, 1, tok],
                                                     exT[:, 2 + n, tok], ALU.is_equal, ALU.mult)
                    last.then_inc(S("one" + L), 1)

            def act_block(n, off=0):
                u, j, g = n // UNIT, n % UNIT, n // GROUP
                if j == 0:
                    dve.wait_ge(S(f"unit{L}{u % 2}"), 32 * (u // 2 + 1) + off * (16 // UNIT))
                x = gin[:, u % 2, j, :]
                hi, lo = a_hi[:, g % 2, n % GROUP, :], a_lo[:, g % 2, n % GROUP, :]
                dve.tensor_tensor(x.rearrange("p (b t) -> p b t", b=NBATCH),
                                  x.rearrange("p (b t) -> p b t", b=NBATCH),
                                  gates[:, u % 2, :, j, :], ALU.mult).then_inc(S("product" + L), 1)
                dve.wait_ge(S("product" + L), 2 * n + 1 + off * 2)
                dve.tensor_copy(hi, x).then_inc(S("product" + L), 1)
                dve.wait_ge(S("product" + L), 2 * n + 2 + off * 2)
                dve.tensor_tensor(lo, x, hi.bitcast(F32), ALU.subtract).then_inc(S("acted" + L), 1)

            def v_tiles(g, first_ada, i=0, turn=0):
                for k in range(GROUP):
                    if turn or g < NGROUP - 1:
                        act_block((g + 1) * GROUP + k, i * 16 if turn else 0)
                    x_update(DENSE[layer] + NKEYS + g * GROUP + k, k, 2 * layer + 1, i * 16 if turn else 0)
                    if layer == 0 and not turn and g == NGROUP - 1 and k:
                        add_square("n1", k - 1)
                    if layer == 0 and k in (1, 3, 5):
                        n = first_ada + k // 2
                        off = i * 6 if turn else 0
                        ada_dot(n, adacol[:, n % 2:n % 2 + 1], off)
                        dve.wait_ge(S("ada_used"), n + 1 + off)
                        dve.tensor_copy(mod[:, 1, ds(n - 4 * DC + off, 1)], adacol[:, n % 2:n % 2 + 1]
                                        ).then_inc(S("ada_col"), 1)
                        dve.wait_ge(S("ada_col"), n - 4 * DC + 1 + off)

            for n in range(GROUP):
                act_block(n)
            v_tiles(0, 4 * DC)
            with dve.Fori(0, V_TURNS) as i:
                for half in range(2):
                    v_tiles(1 + half, 4 * DC + 3 + 3 * half, i, 1)
            for g in range(1 + 2 * V_TURNS, NGROUP):
                v_tiles(g, 4 * DC + 3 * g)

        output(0)
        peer(0)

        add_square("n1", DC - 1)
        root("n1")
        link(dve.tensor_tensor(mod[:, 1, :], mod[:, 1, :], adab[:, 1, :], ALU.add))
        columns(2, 1, 0)
        columns(3, 1, 3 * DC)
        dve.tensor_scalar(g1p[:, 2, :], mod[:, 1, 2 * DC:3 * DC], 1.0, None, ALU.add)
        link(dve.tensor_scalar(g1p[:, 3, :], mod[:, 1, 5 * DC:6 * DC], 1.0, None, ALU.add))
        norm("n1", 2, 1, 0)
        for m in range(2 * DC):
            dve.wait_ge(S("qk_ss"), m + 1)
            dve.tensor_scalar(qrs[:], misc[2 + m % 2][:], 1.0 / HD, EPS, ALU.mult, ALU.add
                              ).then_inc(S("qk_var"), 1)
            dve.wait_ge(S("qk_std"), m + 1)
            link(dve.reciprocal(qrs[:], qrs[:]))
            which, k = divmod(m, DC)
            dve.scalar_tensor_tensor(out=(aq, ak)[which][:, k, :], in0=qf[:, m % 2, :],
                                     scalar=qkn[:, which:which + 1], in1=qrs[:], op0=ALU.mult, op1=ALU.mult
                                     ).then_inc(S("qk_done"), 1)
            dve.wait_ge(S("qk_done"), m + 1)

        def sticks(h):
            if h >= 2:
                dve.wait_ge(S("sp_lo"), CH * (h - 1))
            for j in range(CH):
                dve.wait_ge(S("z"), CH * h + together[j])
                dve.tensor_scalar(sp[:, h % 2, j, j * P:].bitcast(U32), zq(h, j, j).bitcast(U32),
                                  NO_SIGN, None, ALU.bitwise_and).then_inc(S("z_abs"), 1)
            for j in range(CH):
                dve.wait_ge(S("z_ln"), CH * h + j + 1)
                dve.scalar_tensor_tensor(out=sp[:, h % 2, j, j * P:], in0=zq(h, j, j), scalar=0.0,
                                         in1=sp[:, h % 2, j, j * P:], op0=ALU.max, op1=ALU.add
                                         ).then_inc(S("sp"), 1)

        def stick_lows(h):
            for j in range(CH):
                dve.wait_ge(S("sp_hi"), CH * h + j + 1)
                dve.tensor_tensor(sp_lo[:, j, j * P:], sp[:, h % 2, j, j * P:], sp_hi[:, j, j * P:].bitcast(F32),
                                  ALU.subtract).then_inc(S("sp_lo"), 1)

        def mixed_low(h):
            o = HD * (h % 2)
            dve.wait_ge(S("o_hi"), h + 1)
            dve.tensor_tensor(h_lo[o:o + HD, h // 2, :], obank(h)[o:o + HD, :],
                              h_hi[o:o + HD, h // 2, :].bitcast(F32), ALU.subtract).then_inc(S("o_lo"), 1)

        sticks(0)
        stick_lows(0)
        for h in range(SB_HEADS):
            if h + 1 < SB_HEADS:
                sticks(h + 1)
            if h:
                mixed_low(h - 1)
            if h + 1 < SB_HEADS:
                stick_lows(h + 1)
        mixed_low(SB_HEADS - 1)
        output(1)
        peer(1)

    ctx.close()


def kernel(**inputs):
    import numpy as np
    import concourse.bacc as bacc
    from concourse.bass_utils import run_bass_kernel_spmd as run

    a = {k: np.asarray(v) for k, v in inputs.items()}

    def tiles(w):
        return w.reshape(DC, P, -1, P).transpose(2, 1, 0, 3).reshape(-1, P, D)

    def expert_tiles(u, v):
        ut = u.reshape(P, NKEYS, DC, P).transpose(1, 3, 2, 0).reshape(NGROUP, GROUP, P, D)
        vt = v.reshape(P, NGROUP, GROUP, DC, P).transpose(1, 3, 0, 2, 4).reshape(NGROUP, DC, P, D)
        return [ut.reshape(-1, P, D), vt.reshape(-1, P, D)]

    def col(v, n=D):
        return v.reshape(n // P, P).T

    w_in = a["l0_w_in"]
    W = HEADS * P
    gate_tile = np.zeros((D, P), w_in.dtype)
    gate_tile[:, 0:HEADS] = w_in[:, 4 * W:4 * W + HEADS]
    gate_tile[:, 32:32 + HEADS] = w_in[:, 4 * W + HEADS:4 * W + 2 * HEADS]
    stream = np.concatenate(
        [tiles(gate_tile), tiles(w_in[:, 0:3 * W]), tiles(w_in[:, 4 * W + 2 * HEADS:]),
         tiles(w_in[:, 3 * W:4 * W]), tiles(a["l0_w_out"]), tiles(a["l0_peer_wq"])] + expert_tiles(a["l0_peer_u"], a["l0_peer_v"]) +
        [tiles(a["l1_w_qkv"]), tiles(a["l1_w_out"]), tiles(a["l1_peer_wq"])] +
        expert_tiles(a["l1_peer_u"], a["l1_peer_v"]))
    data = {
        "stream": stream,
        "x_t": a["x"].reshape(SEQ, DC, P).transpose(2, 1, 0),
        "c": a["c"].reshape(D),
        "ada": np.concatenate([a[f"l{l}_ada_w"].T.reshape(ADA, P, D) for l in range(2)]),
        "ada_b": np.stack([col(a[f"l{l}_ada_b"], ADA * P) for l in range(2)], 1),
        "gains": np.stack([col(a[n]) for n in ("l0_norm_mix", "l0_norm_ffn", "l1_norm_mix", "l1_norm_ffn")], 1),
        "gate_b": np.stack([a["l0_b_igate"], a["l0_b_fgate"]], 1),
        "conv_w": a["l0_conv_w"].reshape(3, HEADS, P).transpose(2, 1, 0),
        "mnorm": col(a["l0_mlstm_norm"], W),
        "keys": np.stack([np.stack([a[f"l{l}_peer_k{n}"].T for n in (1, 2)], 1) for l in range(2)], 1),
        "qk_norm": np.stack([np.concatenate([a[n], a[n]]) for n in ("l1_q_norm", "l1_k_norm")], 1),
    }
    data = {k: np.ascontiguousarray(v) for k, v in data.items()}
    nc = bacc.Bacc("TRN2", target_bir_lowering=False, num_devices=1)
    args = [nc.dram_tensor(k + "_dram", v.shape, F32, kind="ExternalInput").ap() for k, v in data.items()]
    out_t = nc.dram_tensor("out_dram", (P, DC, SEQ), F32, kind="ExternalOutput").ap()
    build(nc, *args, out_t)
    r = run(nc, [{k + "_dram": v for k, v in data.items()}], core_ids=[0])
    return r.results[0]["out_dram"].transpose(2, 1, 0).reshape(1, SEQ, D)
```
